# Optimizing a Trainium2 kernel written in Bass

```python
import jax, jax.numpy as jnp
from jax import lax
import numpy as np

D_MODEL = 1024
BATCH = 1
SEQ = 1024
DEPTH = 1

CHUNK = 64
EPS = 1e-6

ATTN_HEADS = 16
ATTN_KV_HEADS = 4
Q_PER_KV = ATTN_HEADS // ATTN_KV_HEADS
HEAD_DIM = 64
ATTN_WIDTH = ATTN_HEADS * HEAD_DIM
KV_WIDTH = ATTN_KV_HEADS * HEAD_DIM
WINDOW = 128
WINDOW_CHUNKS = (WINDOW + CHUNK - 1) // CHUNK
BAND = WINDOW_CHUNKS * CHUNK
ROPE_THETA = 10000.0

SSD_EXPAND = 2
SSD_WIDTH = SSD_EXPAND * D_MODEL
SSD_HEAD_DIM = 64
SSD_HEADS = SSD_WIDTH // SSD_HEAD_DIM
SSD_GROUPS = 4
HEADS_PER_GROUP = SSD_HEADS // SSD_GROUPS
SSD_STATE = 128
CONV_WIDTH = 4
CONV_CHANNELS = SSD_WIDTH + 2 * SSD_GROUPS * SSD_STATE

IN_SIZES = (ATTN_WIDTH, KV_WIDTH, KV_WIDTH, ATTN_WIDTH, SSD_WIDTH, CONV_CHANNELS, SSD_HEADS, 2 * D_MODEL)
IN_WIDTH = 2 * ATTN_WIDTH + 2 * KV_WIDTH + SSD_WIDTH + CONV_CHANNELS + SSD_HEADS + 2 * D_MODEL

kernel_name = "hybrid_swa_sink_ssd_gated_merge"

def rms_norm(x, gain):
    xf = x.astype(jnp.float32)
    y = xf * lax.rsqrt(jnp.mean(xf * xf, axis=-1, keepdims=True) + EPS)
    return (y * gain.astype(jnp.float32)).astype(x.dtype)

def apply_rope(t, pos):
    half = HEAD_DIM // 2
    inv_freq = ROPE_THETA ** (-jnp.arange(half, dtype=jnp.float32) / half)
    ang = pos[:, None] * inv_freq[None, :]
    cos = jnp.cos(ang)[None, :, None, :]
    sin = jnp.sin(ang)[None, :, None, :]
    tf = t.astype(jnp.float32)
    t1, t2 = tf[..., :half], tf[..., half:]
    out = jnp.concatenate([t1 * cos - t2 * sin, t2 * cos + t1 * sin], axis=-1)
    return out.astype(t.dtype)

def band_blocks(t, n_chunks):
    b, _, h, d = t.shape
    pad = (WINDOW_CHUNKS - 1) * CHUNK
    tp = jnp.pad(t, ((0, 0), (pad, 0), (0, 0), (0, 0)))
    tc = tp.reshape(b, n_chunks + WINDOW_CHUNKS - 1, CHUNK, h, d)
    return jnp.concatenate([tc[:, j:j + n_chunks] for j in range(WINDOW_CHUNKS)], axis=2)

def window_attention(q, k, v, q_gain, k_gain, sinks):
    b, s, _ = q.shape
    nc = s // CHUNK
    pos = jnp.arange(s, dtype=jnp.float32)
    q = apply_rope(rms_norm(q.reshape(b, s, ATTN_HEADS, HEAD_DIM), q_gain), pos)
    k = apply_rope(rms_norm(k.reshape(b, s, ATTN_KV_HEADS, HEAD_DIM), k_gain), pos)
    v = v.reshape(b, s, ATTN_KV_HEADS, HEAD_DIM)
    q = q.reshape(b, nc, CHUNK, ATTN_KV_HEADS, Q_PER_KV, HEAD_DIM)
    k_band = band_blocks(k, nc)
    v_band = band_blocks(v, nc)
    scores = jnp.einsum('bclkgd,bcmkd->bckglm', q, k_band).astype(jnp.float32) * (HEAD_DIM ** -0.5)
    kpos = jnp.arange(nc)[:, None] * CHUNK - (WINDOW_CHUNKS - 1) * CHUNK + jnp.arange(BAND)[None, :]
    valid = (kpos >= 0)[None, :, None, None, None, :]
    scores = jnp.where(valid, scores, -jnp.inf)
    sink = sinks.astype(jnp.float32).reshape(1, 1, ATTN_KV_HEADS, Q_PER_KV, 1, 1)
    m = jnp.maximum(jnp.max(scores, axis=-1, keepdims=True), sink)
    p = jnp.exp(scores - m)
    probs = p / (jnp.sum(p, axis=-1, keepdims=True) + jnp.exp(sink - m))
    o = jnp.einsum('bckglm,bcmkd->bclkgd', probs.astype(v.dtype), v_band)
    return o.reshape(b, s, ATTN_WIDTH)

def ssd_mixer(xbc, dt_raw, conv_w, conv_b, dt_bias, a_log, d_skip):
    b, s, _ = xbc.shape
    nc = s // CHUNK
    gn = SSD_GROUPS * SSD_STATE
    xbc = lax.conv_general_dilated(
        xbc, conv_w[:, None, :].astype(xbc.dtype), window_strides=(1,),
        padding=[(CONV_WIDTH - 1, 0)], dimension_numbers=('NWC', 'WIO', 'NWC'),
        feature_group_count=CONV_CHANNELS)
    xbc = jax.nn.silu(xbc + conv_b.astype(xbc.dtype))
    xs, bm, cm = jnp.split(xbc, [SSD_WIDTH, SSD_WIDTH + gn], axis=-1)
    xs = xs.reshape(b, nc, CHUNK, SSD_GROUPS, HEADS_PER_GROUP, SSD_HEAD_DIM)
    bm = bm.reshape(b, nc, CHUNK, SSD_GROUPS, SSD_STATE)
    cm = cm.reshape(b, nc, CHUNK, SSD_GROUPS, SSD_STATE)
    dt = jax.nn.softplus(dt_raw.astype(jnp.float32) + dt_bias.astype(jnp.float32))
    dt = dt.reshape(b, nc, CHUNK, SSD_GROUPS, HEADS_PER_GROUP)
    a = -jnp.exp(a_log.astype(jnp.float32)).reshape(SSD_GROUPS, HEADS_PER_GROUP)
    a_cs = jnp.cumsum(dt * a, axis=2)
    causal = jnp.tril(jnp.ones((CHUNK, CHUNK), dtype=bool))[:, :, None, None]
    seg = a_cs[:, :, :, None] - a_cs[:, :, None, :]
    decay = jnp.exp(jnp.where(causal, seg, -jnp.inf))
    cb = jnp.einsum('bclgn,bcsgn->bclsg', cm, bm).astype(jnp.float32)
    w = cb[..., None] * decay * dt[:, :, None]
    y_diag = jnp.einsum('bclsgh,bcsghp->bclghp', w, xs.astype(jnp.float32))
    decay_to_end = jnp.exp(a_cs[:, :, -1:] - a_cs)
    chunk_states = jnp.einsum('bcsgn,bcsgh,bcsghp->bcghpn', bm.astype(jnp.float32),
                              decay_to_end * dt, xs.astype(jnp.float32))
    chunk_decay = jnp.exp(a_cs[:, :, -1])

    def step(carry, inp):
        st, dec = inp
        return carry * dec[..., None, None] + st, carry

    init = jnp.zeros((b, SSD_GROUPS, HEADS_PER_GROUP, SSD_HEAD_DIM, SSD_STATE), jnp.float32)
    _, prev = lax.scan(step, init, (jnp.moveaxis(chunk_states, 1, 0), jnp.moveaxis(chunk_decay, 1, 0)))
    prev = jnp.moveaxis(prev, 0, 1)
    y_off = jnp.einsum('bclgn,bcghpn,bclgh->bclghp', cm.astype(jnp.float32), prev, jnp.exp(a_cs))
    d = d_skip.astype(jnp.float32).reshape(SSD_GROUPS, HEADS_PER_GROUP)[:, :, None]
    y = y_diag + y_off + d * xs.astype(jnp.float32)
    return y.reshape(b, s, SSD_WIDTH).astype(xbc.dtype)

def setup_inputs(seed: int = 0) -> dict:
    key = jax.random.key(seed)
    ks = jax.random.split(key, 20)
    f32 = jnp.float32
    x = jax.random.normal(ks[0], (BATCH, SEQ, D_MODEL), f32)
    norm_gain = 1.0 + 0.02 * jax.random.normal(ks[1], (DEPTH, D_MODEL), f32)
    w_in = jax.random.normal(ks[2], (DEPTH, D_MODEL, IN_WIDTH), f32) * D_MODEL ** -0.5
    b_gate = 0.02 * jax.random.normal(ks[3], (DEPTH, 2 * D_MODEL), f32)
    q_norm_gain = 1.0 + 0.02 * jax.random.normal(ks[4], (DEPTH, HEAD_DIM), f32)
    k_norm_gain = 1.0 + 0.02 * jax.random.normal(ks[5], (DEPTH, HEAD_DIM), f32)
    attn_sinks = 0.5 * jax.random.normal(ks[6], (DEPTH, ATTN_HEADS), f32)
    w_attn_proj = jax.random.normal(ks[7], (DEPTH, ATTN_WIDTH, D_MODEL), f32) * ATTN_WIDTH ** -0.5
    conv_w = jax.random.normal(ks[8], (DEPTH, CONV_WIDTH, CONV_CHANNELS), f32) * CONV_WIDTH ** -0.5
    conv_b = 0.02 * jax.random.normal(ks[9], (DEPTH, CONV_CHANNELS), f32)
    dt0 = jnp.exp(jax.random.uniform(ks[10], (DEPTH, SSD_HEADS), f32, np.log(1e-3), np.log(1e-1)))
    dt_bias = dt0 + jnp.log(-jnp.expm1(-dt0))
    a_log = jnp.log(jax.random.uniform(ks[11], (DEPTH, SSD_HEADS), f32, 1.0, 16.0))
    d_skip = 1.0 + 0.1 * jax.random.normal(ks[12], (DEPTH, SSD_HEADS), f32)
    ssd_norm_gain = 1.0 + 0.02 * jax.random.normal(ks[13], (DEPTH, SSD_WIDTH), f32)
    w_ssd_proj = jax.random.normal(ks[14], (DEPTH, SSD_WIDTH, D_MODEL), f32) * SSD_WIDTH ** -0.5
    w_out = jax.random.normal(ks[15], (DEPTH, D_MODEL, D_MODEL), f32) * D_MODEL ** -0.5
    return {"x": x, "norm_gain": norm_gain, "w_in": w_in, "b_gate": b_gate,
            "q_norm_gain": q_norm_gain, "k_norm_gain": k_norm_gain, "attn_sinks": attn_sinks,
            "w_attn_proj": w_attn_proj, "conv_w": conv_w, "conv_b": conv_b, "dt_bias": dt_bias,
            "a_log": a_log, "d_skip": d_skip, "ssd_norm_gain": ssd_norm_gain,
            "w_ssd_proj": w_ssd_proj, "w_out": w_out}

def reference(x, norm_gain, w_in, b_gate, q_norm_gain, k_norm_gain, attn_sinks, w_attn_proj,
              conv_w, conv_b, dt_bias, a_log, d_skip, ssd_norm_gain, w_ssd_proj, w_out):
    offsets = [int(o) for o in np.cumsum(IN_SIZES)[:-1]]
    for i in range(DEPTH):
        h = rms_norm(x, norm_gain[i])
        proj = h @ w_in[i].astype(h.dtype)
        q, k, v, z_a, z_s, xbc, dt_raw, gate_pre = jnp.split(proj, offsets, axis=-1)
        o_a = window_attention(q, k, v, q_norm_gain[i], k_norm_gain[i], attn_sinks[i])
        branch_a = (o_a * jax.nn.silu(z_a)) @ w_attn_proj[i].astype(h.dtype)
        y_s = ssd_mixer(xbc, dt_raw, conv_w[i], conv_b[i], dt_bias[i], a_log[i], d_skip[i])
        y_s = rms_norm(y_s * jax.nn.silu(z_s), ssd_norm_gain[i])
        branch_b = y_s @ w_ssd_proj[i].astype(h.dtype)
        gates = jax.nn.sigmoid((gate_pre + b_gate[i].astype(h.dtype)).astype(jnp.float32)).astype(h.dtype)
        g_a, g_b = jnp.split(gates, 2, axis=-1)
        merged = g_a * branch_a + g_b * branch_b
        x = x + merged @ w_out[i].astype(h.dtype)
    return x


_drawn_inputs = setup_inputs


def setup_inputs(seed=0):
    import zlib

    import numpy as np

    out = dict(_drawn_inputs(seed))
    spreads = {}
    factors = {'norm_gain': 3.531,
     'b_gate': 8.0,
     'q_norm_gain': 8.0,
     'k_norm_gain': 8.0,
     'attn_sinks': 8.0,
     'conv_b': 14.408,
     'ssd_norm_gain': 29.4,
     'd_skip': 8.0}
    for name, (base, spread) in spreads.items():
        noise = np.random.default_rng([zlib.crc32(name.encode()), seed]).standard_normal(out[name].shape)
        drawn = base * np.exp(spread * noise) if base else spread * noise
        out[name] = __import__('jax').numpy.asarray(drawn.astype(out[name].dtype))
    for name, factor in factors.items():
        out[name] = (out[name] * factor).astype(out[name].dtype)
    return out
```

```python
import concourse.bass as bass
from concourse import mybir
from contextlib import ExitStack

P = 128
T = 1024
DM = 1024
NT = T // P
NK = DM // P
HALF = T // 2
CH = 64
HD = 64
NH = 16
NKV = 4
GROUPS = 4
HG = 8
NHS = GROUPS * HG
V0, K0, Q0, X0U, Z0 = 1, 3, 5, 13, 37
B2, B3, UNITS = 45, 77, 109
NX = 24
EPS = 1e-6
NEG = -1e30

CONST_COLS = [("b_gate", 16), ("ssd_gain", 16), ("d_skip", 16), ("sinks", NH), ("pad_mask", NT), ("ident", P), ("tri", P),
              ("ones", P), ("conv_w", NX * 4), ("conv_b", NX), ("q_gain", 1), ("k_gain", 1), ("dt_bias", NHS),
              ("a_log", NHS), ("head_ones", P), ("head_sel", 2)]
CONST_AT = {}
_at = 0
for _n, _w in CONST_COLS:
    CONST_AT[_n] = (_at, _at + _w)
    _at += _w
NCONST = _at
BLOCK1_CONSTS = CONST_AT["conv_w"][0]


class Chain:

    def __init__(self, eng, sem):
        self.eng, self.sem, self.n = eng, sem, 0

    def link(self, ins):
        ins.then_inc(self.sem, 1)
        self.n = self.n + 1
        self.eng.wait_ge(self.sem, self.n)

    def loop(self, eng_loop, count, steps):
        base = self.n
        with eng_loop(0, count) as i:
            self.n = i * steps + base
            self.k = 0
            yield i
        self.n = base + count * steps


SCRATCH = "Internal"


def build(nc, a, out):
    f32, f32r = mybir.dt.float32, mybir.dt.float32r
    ALU, ACT, AX = mybir.AluOpType, mybir.ActivationFunctionType, mybir.AxisListType
    ds = bass.ds

    def dram(name, shape):
        return nc.dram_tensor(name, shape, f32, kind=SCRATCH).ap()

    q_d = dram("q_d", (8, P, T))
    k_d = dram("k_d", (2, P, CH + T))
    v_d = dram("v_d", (CH + T, NKV * HD))
    x_d = dram("x_d", (NX, P, T))
    z_d = dram("z_d", (24, P, T))
    g_d = dram("g_d", (16, P, T))
    cs_d = dram("cs_d", (NHS, T))
    o_d = dram("o_d", (8, P, T))
    y_d = dram("y_d", (16, P, T))
    a_d = dram("a_d", (8, P, T))

    root = ExitStack()
    with root:
        def sbuf(ctx, name, shape, dt=f32):
            return ctx.enter_context(nc.sbuf_tensor("sb_" + name, shape, dt))

        def sems(ctx, *names):
            return [ctx.enter_context(nc.semaphore(n)) for n in names]

        cst = sbuf(root, "cst", [P, BLOCK1_CONSTS])
        const_tiles = [(0, cst)]

        def C(name, lo=0, hi=None):
            b, e = CONST_AT[name]
            first, tile = const_tiles[b >= BLOCK1_CONSTS]
            return tile[:, b - first + lo:(e if hi is None else b + hi) - first]

        wst = sbuf(root, "wst", [P, 2, NK, P])
        whl = sbuf(root, "whl", [P, 2, 2, NK, P], f32r)
        ssd_sb = sbuf(root, "ssd_sb", [P, 5, NT, NHS])
        dt_sb = ssd_sb[:, 0]
        cs_sb = ssd_sb[:, 1]
        ecs_sb = ssd_sb[:, 2]
        cd_sb = ssd_sb[:, 3]
        de_sb = ssd_sb[:, 4]
        rq_sb = sbuf(root, "rq_sb", [P, NT, NH])
        eps = sbuf(root, "eps", [P, 1])
        X0 = sbuf(root, "X0", [P, 2, NK, T], f32r)

        def flat(ap):
            return ap.rearrange("p a b -> p (a b)")

        def matmuls(bank, slot, act, half):
            for k in range(NK):
                for wp, ap in ((0, 0), (0, 1), (1, 0)):
                    last = nc.tensor.matmul(bank, whl[:, slot, wp, k, :],
                                            act[:, ap, k, half * HALF:(half + 1) * HALF],
                                            start=(k == 0 and wp == 0 and ap == 0),
                                            stop=(k == NK - 1 and wp == 1))
            return last

        def split_high(slot):
            return nc.scalar.activation(whl[:, slot, 0], wst[:, slot], ACT.Copy)

        def split_low(slot):
            return nc.gpsimd.tensor_tensor(whl[:, slot, 1], wst[:, slot], whl[:, slot, 0].bitcast(f32), ALU.subtract)

        w_in = sems(root, "w_in0", "w_in1")
        w_hi, w_lo, unit_done = sems(root, "w_hi", "w_lo", "unit_done")

        def load_w(sp, u, c, at):
            if u >= 2:
                sp.wait_ge(w_hi, at * c + (u - 1))
                sp.wait_ge(w_lo, at * c + (u - 1))
            src = a["w_units"][ds(at * c + u, 1)] if c else a["w_units"][u:u + 1]
            sp.dma_start(wst[:, u % 2].rearrange("p k c -> p (k c)"), src.rearrange("a p c -> (a p) c")).then_inc(w_in[u % 2], 16)

        def high(act, u, c, at):
            act.wait_ge(w_in[u % 2], at * (8 * c) + 16 * (u // 2 + 1))
            if u >= 2:
                act.wait_ge(unit_done, at * (2 * c) + 2 * (u - 1))
            split_high(u % 2).then_inc(w_hi, 1)

        def low(pool, u, c, at):
            pool.wait_ge(w_hi, at * c + (u + 1))
            split_low(u % 2).then_inc(w_lo, 1)

        with ExitStack() as ctx:
            cst1 = sbuf(ctx, "cst1", [P, NCONST - BLOCK1_CONSTS])
            const_tiles.append((BLOCK1_CONSTS, cst1))
            xrow = sbuf(ctx, "xrow", [P, NT, DM])
            gain = sbuf(ctx, "gain", [P, DM])
            cos = sbuf(ctx, "cos", [P, T])
            sin = sbuf(ctx, "sin", [P, T])
            staged = xrow
            krms = xrow[:, 3:5, :]
            res = sbuf(ctx, "res", [P, 2, T])
            cv = sbuf(ctx, "cv", [P, 2, T])
            gq = sbuf(ctx, "gq", [P, 2, T])
            sq = sbuf(ctx, "sq", [P, 2, T])
            ssx = sbuf(ctx, "ssx", [P, 2, NT])
            small = sbuf(ctx, "small", [P, 6, NT, NHS])
            neg_a = sbuf(ctx, "neg_a", [P, NHS])
            csT = sbuf(ctx, "csT", [NHS, T])
            zpad = sbuf(ctx, "zpad", [P, 256])
            F = ctx.enter_context(nc.psum_tensor("F1", [P, 4, 512], f32))
            M = ctx.enter_context(nc.psum_tensor("M1", [P, 4, 512], f32))
            (consts_in, gain_in, rope_in, x_sq, x_rt, xn_ready, xt_done, x_hi, x_lo, dve_step, dt_staged, dtT_done,
             dt_z, dt_e, dt_w, dt_l, dA_ready, cs_done, cs_a, v_staged, vT_done, v_ready, pads_set, pads_in,
             csT_done, csT_ready, cs_stored, gq_ready, rope_done, kss_done, k_rt, ssq_done, conv_done, silu_done,
             qst_rt, z_taken, gq_free) = sems(
                ctx, "consts_in", "gain_in", "rope_in", "x_sq", "x_rt", "xn_ready", "xt_done", "x_hi", "x_lo",
                "dve_step", "dt_staged", "dtT_done", "dt_z", "dt_e", "dt_w", "dt_l", "dA_ready", "cs_done", "cs_a",
                "v_staged", "vT_done", "v_ready", "pads_set", "pads_in", "csT_done", "csT_ready", "cs_stored",
                "gq_ready", "rope_done", "kss_done", "k_rt", "ssq_done", "conv_done", "silu_done", "qst_rt",
                "z_taken", "gq_free")
            x_in = sems(ctx, *[f"x_in{i}" for i in range(NT)])
            pair_free = sems(ctx, "pair_free0", "pair_free1")
            stored = sems(ctx, "stored0", "stored1")

            def pair(p):
                return F[:, 2 * p:2 * p + 2, :].rearrange("p b c -> p (b c)")

            def x_banks(i):
                return (M[:, 0:2, :], M[:, 2:4, :], F[:, 2:4, :])[i % 3]

            block = ctx.enter_context(nc.Block())

            @block.sync
            def _(sp):
                for i in range(NT):
                    sp.dma_start(xrow[:, i, :], a["x"][i * P:(i + 1) * P, :]).then_inc(x_in[i], 16)
                    if i == 3:
                        load_w(sp, 0, 0, 0)
                load_w(sp, 1, 0, 0)
                sp.dma_start(cos[:, :], a["cos"]).then_inc(rope_in, 16)
                sp.dma_start(sin[:, :], a["sin"]).then_inc(rope_in, 16)
                for u in range(2, Q0 + 4):
                    load_w(sp, u, 0, 0)
                for u in (K0, K0 + 1):
                    sp.wait_ge(rope_done, u - K0 + 1)
                    sp.dma_start(k_d[u - K0, :, CH:], res[:, u % 2, :]).then_inc(stored[u % 2], 16)
                with nc.sync.Fori(0, 4) as i:
                    for s in range(2):
                        load_w(sp, Q0 + 4 + s, 2, i)
                        sp.wait_ge(rope_done, i * 2 + (3 + s))
                        sp.dma_start(q_d[ds(i * 2 + s, 1), :, :], res[:, (Q0 + s) % 2, :]).then_inc(stored[(Q0 + s) % 2], 16)
                with nc.sync.Fori(0, (B2 + 2 - Q0 - 12) // 2) as i:
                    for n in range(2):
                        load_w(sp, Q0 + 12 + n, 2, i)

            @block.gpsimd
            def _(pool):
                nc.gpsimd.memset(zpad[:], 0.0).then_inc(pads_set, 1)
                pool.wait_ge(pads_set, 1)
                for kt in range(2):
                    pool.dma_start(k_d[kt, :, 0:CH], zpad[:, 0:CH]).then_inc(pads_in, 16)
                pool.dma_start(v_d[0:CH, :], zpad[0:CH, :]).then_inc(pads_in, 16)

                low(pool, 0, 0, 0)
                with nc.gpsimd.Fori(0, (B2 + 1) // 2) as i:
                    for n in range(2):
                        low(pool, 1 + n, 2, i)
                pool.wait_ge(pads_in, 48)

            @block.scalar
            def _(act):
                act.dma_start(cst[:, :], a["consts"][:, 0:BLOCK1_CONSTS]).then_inc(consts_in, 16)
                act.dma_start(cst1[:, :], a["consts"][:, BLOCK1_CONSTS:]).then_inc(consts_in, 16)
                act.dma_start(gain[:, :], a["gain"]).then_inc(gain_in, 16)
                act.wait_ge(dve_step, 1)
                act.sem_inc(silu_done, 2)

                def x_high(i):
                    act.wait_ge(xt_done, i + 1)
                    nc.scalar.activation(X0[:, 0, :, i * P:(i + 1) * P], x_banks(i).rearrange("p b (k t) -> p (b k) t", t=P),
                                         ACT.Copy).then_inc(x_hi, 1)

                for i in range(NT):
                    act.wait_ge(x_in[i], 16)
                    nc.scalar.activation(cv[:, 0, :], xrow[:, i, :], ACT.Square, accum_out=ssx[:, 0, i:i + 1]).then_inc(x_sq, 1)
                    act.wait_ge(x_sq, i + 1)
                    nc.scalar.activation(ssx[:, 0, i:i + 1], ssx[:, 0, i:i + 1], ACT.Sqrt, bias=eps[:], scale=1.0 / DM).then_inc(x_rt, 1)
                    if i >= 1:
                        x_high(i - 1)
                    if i == 4:
                        high(act, 0, 0, 0)
                x_high(NT - 1)
                high(act, 1, 0, 0)

                act.wait_ge(consts_in, 32)
                nc.scalar.activation(neg_a[:], C("a_log"), ACT.Exp)
                act.wait_ge(unit_done, 2)
                nc.scalar.activation(staged[0:NHS, 0, :], pair(0)[0:NHS, :], ACT.Copy).then_inc(pair_free[0], 1)
                high(act, 2, 0, 0)

                def stage_v(u):
                    act.wait_ge(unit_done, 2 * u + 2)
                    nc.scalar.activation(staged[:, u, :], pair(u % 2), ACT.Copy).then_inc(pair_free[u % 2], 1)
                    high(act, u + 2, 0, 0)

                def v_out(u, b):
                    act.wait_ge(vT_done, u)
                    nc.scalar.activation(res[:, u % 2, :], flat(M[:, b:b + 2, :]), ACT.Copy).then_inc(v_ready, 1)
                    act.wait_ge(v_ready, u)
                    act.dma_start(v_d[CH:, (u - V0) * P:(u - V0 + 1) * P].rearrange("(t p) c -> p t c", p=P),
                                  res[:, u % 2, :].rearrange("p (t c) -> p t c", t=NT)).then_inc(stored[u % 2], 16)

                stage_v(V0)
                act.wait_ge(dt_z, 1)
                nc.scalar.activation(small[:, 1], small[:, 1], ACT.Exp).then_inc(dt_e, 1)
                act.wait_ge(dt_w, 1)
                nc.scalar.activation(small[:, 4], small[:, 2], ACT.Ln).then_inc(dt_l, 1)
                stage_v(V0 + 1)
                v_out(V0, 2)
                act.wait_ge(cs_a, 1)
                nc.scalar.activation(ecs_sb, cs_sb, ACT.Exp)
                nc.scalar.activation(de_sb, small[:, 5], ACT.Exp)
                nc.scalar.activation(cd_sb, small[:, 0], ACT.Exp)
                v_out(V0 + 1, 0)
                act.wait_ge(csT_done, 1)
                nc.scalar.activation(csT[:, :], M[0:NHS, 2:4, :].rearrange("p b c -> p (b c)"), ACT.Copy).then_inc(csT_ready, 1)
                act.wait_ge(csT_ready, 1)
                act.dma_start(cs_d[:, :], csT[:, :]).then_inc(cs_stored, 16)

                def gain_and_square(p, g, done):
                    for h in range(2):
                        act.wait_ge(unit_done, done + h)
                        to = slice(h * HALF, (h + 1) * HALF)
                        nc.scalar.activation(gq[:, p, to], F[:, 2 * p + h, :], ACT.Identity, scale=C(g)).then_inc(gq_ready, 1)
                        last = nc.scalar.activation(sq[:, p, to], F[:, 2 * p + h, :], ACT.Square)
                    last.then_inc(pair_free[p], 1)

                for u in (K0, K0 + 1):
                    gain_and_square(u % 2, "k_gain", 2 * u + 1)
                    high(act, u + 2, 0, 0)
                for u in (K0, K0 + 1):
                    act.wait_ge(kss_done, u - K0 + 1)
                    b = 2 * (u - K0)
                    nc.scalar.activation(krms[:, u - K0, :], M[:, b:b + 2, :].rearrange("p b c -> p (b c)"), ACT.Sqrt,
                                         bias=eps[:], scale=1.0 / HD).then_inc(k_rt, 1)
                with nc.scalar.Fori(0, 4) as i:
                    for s in range(2):
                        p = (Q0 + s) % 2
                        act.wait_ge(ssq_done, i * 2 + (1 + s))
                        act.wait_ge(gq_free, i * 2 + (1 + s))
                        gain_and_square(p, "q_gain", i * 4 + (2 * (Q0 + s) + 1))
                        high(act, Q0 + s + 2, 2, i)
                act.wait_ge(ssq_done, 10)
                nc.scalar.activation(rq_sb[:].rearrange("p t (b u i) -> p (t b) u i", b=2, u=2),
                                     M[:, 0, 0:NT * NH].rearrange("p (tb i u) -> p tb u i", i=4, u=2), ACT.Sqrt,
                                     bias=eps[:], scale=1.0 / HD).then_inc(qst_rt, 1)
                with nc.scalar.Fori(0, NX // 2) as i:
                    for s in range(2):
                        p = (X0U + s) % 2
                        high(act, X0U + s + 2, 2, i)
                        act.wait_ge(conv_done, i * 2 + (s + 1))
                        act.wait_ge(stored[p], i * 16 + 16 * ((X0U + s - 1) // 2))
                        nc.scalar.activation(res[:, p, :], cv[:, p, :], ACT.Silu, bias=C("conv_b")[:, ds(i * 2 + s, 1)]).then_inc(silu_done, 1)
                        act.wait_ge(silu_done, i * 2 + (s + 3))
                        act.dma_start(x_d[ds(i * 2 + s, 1), :, :], res[:, p, :]).then_inc(stored[p], 16)

                with nc.scalar.Fori(0, 4) as i:
                    for s in range(2):
                        p = (Z0 + s) % 2
                        act.wait_ge(unit_done, i * 4 + (2 * (Z0 + s) + 2))
                        act.wait_ge(stored[p], i * 16 + 16 * ((Z0 + s - 1) // 2))
                        nc.scalar.activation(res[:, p, :], pair(p), ACT.Silu).then_inc(z_taken, 1)
                        high(act, Z0 + s + 2, 2, i)
                        act.wait_ge(z_taken, i * 2 + (s + 1))
                        act.sem_inc(pair_free[p], 1)
                        act.dma_start(z_d[ds(i * 2 + s, 1), :, :], res[:, p, :]).then_inc(stored[p], 16)
                for p in range(2):
                    act.wait_ge(stored[p], 16 * 22)
                act.wait_ge(cs_stored, 16)

            @block.vector
            def _(dve):
                ch = Chain(dve, dve_step)
                ch.link(nc.vector.memset(eps[:], EPS))

                def x_low(i):
                    dve.wait_ge(x_hi, i + 1)
                    to = slice(i * P, (i + 1) * P)
                    nc.vector.tensor_tensor(X0[:, 1, :, to], x_banks(i).rearrange("p b (k t) -> p (b k) t", t=P),
                                            X0[:, 0, :, to].bitcast(f32), ALU.subtract).then_inc(x_lo, 1)

                dve.wait_ge(gain_in, 16)
                for i in range(NT):
                    dve.wait_ge(x_rt, i + 1)
                    ch.link(nc.vector.reciprocal(ssx[:, 1, i:i + 1], ssx[:, 0, i:i + 1]))
                    nc.vector.scalar_tensor_tensor(xrow[:, i, :], xrow[:, i, :], ssx[:, 1, i:i + 1], gain[:],
                                                   ALU.mult, ALU.mult).then_inc(xn_ready, 1)
                    if i >= 1:
                        x_low(i - 1)
                x_low(NT - 1)

                z, e, w, d, ln, t5 = (small[:, n] for n in range(6))

                def per_tile(name):
                    return C(name).unsqueeze(1).to_broadcast([P, NT, NHS])

                dve.wait_ge(dtT_done, 1)
                dve.wait_ge(consts_in, 32)
                ch.link(nc.vector.tensor_tensor(z, M[:, 0, 0:NT * NHS].rearrange("p (t h) -> p t h", t=NT), per_tile("dt_bias"), ALU.add))
                nc.vector.scalar_tensor_tensor(e, z, -1.0, z, ALU.mult, ALU.min).then_inc(dt_z, 1)
                dve.wait_ge(dt_e, 1)
                ch.link(nc.vector.tensor_scalar(w, e, 1.0, None, ALU.add))
                dve.sem_inc(dt_w, 1)
                ch.link(nc.vector.tensor_scalar(d, w, 1.0, None, ALU.subtract))
                ch.link(nc.vector.tensor_scalar(t5, d, 0.0, None, ALU.is_equal))
                ch.link(nc.vector.tensor_tensor(d, d, t5, ALU.add))
                ch.link(nc.vector.reciprocal(d, d))
                ch.link(nc.vector.tensor_tensor(d, d, e, ALU.mult))
                dve.wait_ge(dt_l, 1)
                ch.link(nc.vector.tensor_tensor(ln, ln, d, ALU.mult))
                ch.link(nc.vector.tensor_tensor(t5, t5, e, ALU.mult))
                ch.link(nc.vector.tensor_tensor(ln, ln, t5, ALU.add))
                ch.link(nc.vector.scalar_tensor_tensor(dt_sb, z, 0.0, ln, ALU.max, ALU.add))
                ch.link(nc.vector.tensor_scalar(neg_a[:], neg_a[:], -1.0, None, ALU.mult))
                nc.vector.tensor_tensor(z, dt_sb, neg_a[:].unsqueeze(1).to_broadcast([P, NT, NHS]), ALU.mult).then_inc(dA_ready, 1)
                dve.wait_ge(cs_done, 1)
                ch.link(nc.vector.tensor_copy(cs_sb, M[:, 0, 0:NT * NHS].rearrange("p (t h) -> p t h", t=NT)))
                ch.link(nc.vector.tensor_copy(z, M[:, 1, 0:NT * NHS].rearrange("p (t h) -> p t h", t=NT)))
                nc.vector.tensor_tensor(t5, z, cs_sb, ALU.subtract).then_inc(cs_a, 1)

                def rotate(p, gq_count, slot_stored, norm=None, steps=4):
                    dve.wait_ge(gq_ready, gq_count)
                    for b in (0, 64):
                        for src, dst in ((b, b + 32), (b + 32, b)):
                            sw = nc.vector.tensor_tensor(cv[dst:dst + 32, p, :], gq[src:src + 32, p, :], sin[src:src + 32, :], ALU.mult)
                    ch.link(sw)
                    dve.wait_ge(stored[p], slot_stored)
                    ch.link(nc.vector.tensor_tensor(res[:, p, :], gq[:, p, :], cos[:], ALU.mult))
                    dve.sem_inc(gq_free, 1)
                    last = nc.vector.tensor_tensor(res[:, p, :], res[:, p, :], cv[:, p, :], ALU.add)
                    if norm is None:
                        last.then_inc(rope_done, 1)
                    else:
                        ch.link(last)

                dve.wait_ge(rope_in, 32)
                for u in (K0, K0 + 1):
                    rotate(u % 2, 2 * (u - K0 + 1), 16 * ((u - 1) // 2), norm=True)
                for u in (K0, K0 + 1):
                    dve.wait_ge(k_rt, u - K0 + 1)
                    ch.link(nc.vector.reciprocal(krms[:, u - K0, :], krms[:, u - K0, :]))
                    nc.vector.tensor_tensor(res[:, u % 2, :], res[:, u % 2, :], krms[:, u - K0, :], ALU.mult).then_inc(rope_done, 1)
                for i in ch.loop(nc.vector.Fori, 4, 4):
                    for s in range(2):
                        rotate((Q0 + s) % 2, i * 4 + (2 * s + 6), i * 16 + 16 * ((Q0 + s - 1) // 2))
                dve.wait_ge(qst_rt, 1)
                ch.link(nc.vector.reciprocal(rq_sb[:], rq_sb[:]))
                nc.vector.tensor_scalar(rq_sb[:], rq_sb[:], HD ** -0.5, None, ALU.mult)
                cw = C("conv_w").rearrange("p (n k) -> p n k", k=4)
                for i in ch.loop(nc.vector.Fori, NX // 2, 6):
                    for s in range(2):
                        p = (X0U + s) % 2
                        acc, raw = cv[:, p, :], pair(p)

                        def tap(k):
                            return cw[:, ds(i * 2 + s, 1), k:k + 1].rearrange("p a b -> p (a b)")

                        dve.wait_ge(unit_done, i * 4 + (2 * (X0U + s) + 2))
                        dve.wait_ge(silu_done, i * 2 + s + 1)
                        ch.link(nc.vector.tensor_scalar(acc, raw, tap(3), None, ALU.mult))
                        for back in (1, 2, 3):
                            ins = nc.vector.scalar_tensor_tensor(acc[:, back:], raw[:, 0:T - back], tap(3 - back), acc[:, back:], ALU.mult, ALU.add)
                            if back < 3:
                                ch.link(ins)
                        ins.then_inc(conv_done, 1)
                        dve.wait_ge(conv_done, i * 2 + (s + 1))
                        dve.sem_inc(pair_free[p], 1)

            @block.tensor
            def _(pe):
                pe.sem_inc(ssq_done, 2)
                pe.wait_ge(consts_in, 32)
                for i in range(NT):
                    pe.wait_ge(xn_ready, i + 1)
                    if i >= 3:
                        pe.wait_ge(x_lo, i - 2)
                    for k in range(NK):
                        last = nc.tensor.transpose(x_banks(i)[:, k // 4, (k % 4) * P:(k % 4 + 1) * P],
                                                   xrow[:, i, k * P:(k + 1) * P], C("ident"))
                    last.then_inc(xt_done, 1)
                    if i == NT // 2:
                        pe.wait_ge(x_lo, NT // 2)
                        pe.wait_ge(w_hi, 1)
                        pe.wait_ge(w_lo, 1)
                        matmuls(F[:, 0, :], 0, X0, 0).then_inc(unit_done, 1)

                def unit(p, hi, free):
                    pe.wait_ge(w_hi, hi)
                    pe.wait_ge(w_lo, hi)
                    if free is not None:
                        pe.wait_ge(pair_free[p], free)
                    for h in range(2):
                        matmuls(F[:, 2 * p + h, :], p, X0, h).then_inc(unit_done, 1)

                def v_rows(u, b):
                    pe.wait_ge(pair_free[u % 2], u // 2 + 1)
                    for t in range(NT):
                        last = nc.tensor.transpose(M[:, b + t // 4, (t % 4) * P:(t % 4 + 1) * P],
                                                   staged[:, u, t * P:(t + 1) * P], C("ident"))
                    last.then_inc(vT_done, 1)

                pe.wait_ge(x_lo, NT)
                matmuls(F[:, 1, :], 0, X0, 1).then_inc(unit_done, 1)
                unit(V0 % 2, V0 + 1, None)
                pe.wait_ge(pair_free[0], 1)
                for t in range(NT):
                    last = nc.tensor.transpose(M[:, 0, t * NHS:(t + 1) * NHS], staged[0:NHS, 0, t * P:(t + 1) * P], C("ident")[0:NHS, 0:NHS])
                last.then_inc(dtT_done, 1)
                unit(0, V0 + 2, 1)
                v_rows(V0, 2)
                pe.wait_ge(dA_ready, 1)
                dA = small[:, 0].rearrange("p t h -> p (t h)")
                nc.tensor.matmul(M[:, 0, 0:NT * NHS], C("tri"), dA, start=True, stop=True)
                nc.tensor.matmul(M[:, 1, 0:NT * NHS], C("ones"), dA, start=True, stop=True).then_inc(cs_done, 1)
                unit(1, K0 + 1, 1)
                pe.wait_ge(cs_a, 1)
                v_rows(V0 + 1, 0)
                pe.wait_ge(v_ready, 1)
                for t in range(NT):
                    last = nc.tensor.transpose(M[0:NHS, 2 + t // 4, (t % 4) * P:(t % 4 + 1) * P], cs_sb[:, t, :], C("ident"))
                last.then_inc(csT_done, 1)
                unit(0, K0 + 2, 2)
                pe.wait_ge(v_ready, 2)
                pe.wait_ge(csT_ready, 1)
                for u in (K0, K0 + 1):
                    pe.wait_ge(pair_free[u % 2], u // 2 + 1)
                    for h in range(2):
                        last = nc.tensor.matmul(M[:, 2 * (u - K0) + h, :], C("head_ones"), sq[:, u % 2, h * HALF:(h + 1) * HALF], start=True, stop=True)
                    last.then_inc(kss_done, 1)
                with nc.tensor.Fori(0, 4) as i:
                    for s in range(2):
                        unit((Q0 + s) % 2, i * 2 + (Q0 + s + 1), i + (Q0 + s) // 2)
                    for s in range(2):
                        p = (Q0 + s) % 2
                        pe.wait_ge(pair_free[p], i + ((Q0 + s) // 2 + 1))
                        if s == 0:
                            pe.wait_ge(k_rt, 2)
                        for t in range(NT):
                            last = nc.tensor.matmul(M[:, 0, ds(i * 4 + (t * NH + 2 * s), 2)], sq[:, p, t * P:(t + 1) * P], C("head_sel"), start=True, stop=True)
                        last.then_inc(ssq_done, 1)
                with nc.tensor.Fori(0, NX // 2) as i:
                    for s in range(2):
                        unit((X0U + s) % 2, i * 2 + (X0U + s + 1), i + (X0U + s) // 2)
                with nc.tensor.Fori(0, 4) as i:
                    for s in range(2):
                        unit((Z0 + s) % 2, i * 2 + (Z0 + s + 1), i + (Z0 + s) // 2)

        with ExitStack() as ctx:
            qs = sbuf(ctx, "qs", [P, 8, P])
            ks = sbuf(ctx, "ks", [P, 2, CH + P])
            vs = sbuf(ctx, "vs", [P, 2, NKV * HD])
            xb = sbuf(ctx, "xb", [P, 16, P])
            bc = sbuf(ctx, "bc", [P, 8, P])
            csb = sbuf(ctx, "csb", [P, NHS, P])
            probs = sbuf(ctx, "probs", [P, 2, 4, P])
            pT = sbuf(ctx, "pT", [P, 2, 4, P])
            negm = sbuf(ctx, "negm", [P, NH])
            stat = sbuf(ctx, "stat", [P, 6, NH])
            orow = sbuf(ctx, "orow", [P, 2, 512])
            zo = sbuf(ctx, "zo", [P, 8, P])
            dec = sbuf(ctx, "dec", [P, 2, HG, P])
            xdt = sbuf(ctx, "xdt", [P, GROUPS, 512])
            xdd = sbuf(ctx, "xdd", [P, GROUPS, 512])
            brow = sbuf(ctx, "brow", [P, GROUPS, P])
            cbm = sbuf(ctx, "cbm", [P, GROUPS, P])
            ytmp = sbuf(ctx, "ytmp", [P, 512])
            yrow = sbuf(ctx, "yrow", [P, 2, 512])
            yo = sbuf(ctx, "yo", [P, 16, P])
            state = sbuf(ctx, "state", [P, GROUPS, 512])
            fres = sbuf(ctx, "fres", [P, 2, T])
            F = ctx.enter_context(nc.psum_tensor("F2", [P, 2, 512], f32))
            S = ctx.enter_context(nc.psum_tensor("S2", [P, 2, 512], f32))
            Tb = ctx.enter_context(nc.psum_tensor("T2", [P, 2, 512], f32))
            O = ctx.enter_context(nc.psum_tensor("O2", [P, 2, 512], f32))
            (sc_done, xr_done, pt_done, pv_done, brt_done, cb_done, ot_done, yg_done, st_done, yt_done) = sems(
                ctx, "sc_done", "xr_done", "pt_done", "pv_done", "brt_done", "cb_done", "ot_done", "yg_done", "st_done",
                "yt_done")
            (step2, negm_ready, sinkm_ready, rsum_ready, xdt_ready, orow_ready, cbm_ready, seg_ready, wT_ready, yrow_ready,
             state_ready, yout_ready) = sems(
                ctx, "step2", "negm_ready", "sinkm_ready", "rsum_ready", "xdt_ready", "orow_ready", "cbm_ready", "seg_ready", "wT_ready",
                "yrow_ready", "state_ready", "yout_ready")
            (probs_ready, sinke_ready, pT_ready, brow_ready, oT_ready, dec_ready, half_taken) = sems(
                ctx, "probs_ready", "sinke_ready", "pT_ready", "brow_ready", "oT_ready", "dec_ready", "half_taken")
            (xd_ready, xdd_ready, sdec_ready) = sems(ctx, "xd_ready", "xdd_ready", "sdec_ready")
            (q_in, k_in, x2_in, v_in, bc_in, cs_in, z_in, o_stored, y_stored) = sems(
                ctx, "q_in", "k_in", "x2_in", "v_in", "bc_in", "cs_in", "z_in", "o_stored", "y_stored")
            f_stored = sems(ctx, "f_stored0", "f_stored1")

            block = ctx.enter_context(nc.Block())

            @block.sync
            def _(sp):
                with nc.sync.Fori(0, NT) as j:
                    at_j = sp.snap(j * P)
                    sp.wait_ge(sc_done, j * 4 + 1)
                    sp.dma_start(qs[:], q_d[:, :, ds(at_j, P)].rearrange("n p t -> p n t")).then_inc(q_in, 16)
                    sp.dma_start(ks[:], k_d[:, :, ds(at_j, CH + P)].rearrange("n p t -> p n t")).then_inc(k_in, 16)
                    sp.wait_ge(xr_done, j * 4 + 1)
                    sp.wait_ge(xd_ready, j * 4 + 1)
                    sp.dma_start(xb[:], x_d[0:16, :, ds(at_j, P)].rearrange("n p t -> p n t")).then_inc(x2_in, 16)
                    sp.wait_ge(pv_done, j * 2 + 1)
                    for half in range(2):
                        sp.dma_start(vs[:, half, :], v_d[ds(at_j + half * CH, P), :]).then_inc(v_in, 16)
                    load_w(sp, B2 + 2, 4, j)
                    sp.wait_ge(yg_done, j * 4 + 1)
                    sp.dma_start(bc[:], x_d[16:24, :, ds(at_j, P)].rearrange("n p t -> p n t")).then_inc(bc_in, 16)
                    sp.wait_ge(seg_ready, j * 4 + 1)
                    sp.dma_start(csb[:], cs_d[:, ds(at_j, P)].partition_broadcast(P)).then_inc(cs_in, 16)
                    sp.wait_ge(o_stored, j * 16 + 16)
                    sp.dma_start(zo[:], z_d[0:8, :, ds(at_j, P)].rearrange("n p t -> p n t")).then_inc(z_in, 16)
                    for n in range(3, 6):
                        load_w(sp, B2 + n, 4, j)

            @block.tensor
            def _(pe):
                for sem, credit in ((sc_done, 1), (xr_done, 1), (pv_done, 1), (yg_done, 1)):
                    pe.sem_inc(sem, credit)
                with nc.tensor.Fori(0, NT) as j:
                    def at(n, k):
                        return j * n + k

                    def scores(r):
                        u = r % 2
                        for c in range(4):
                            for half in range(2):
                                last = nc.tensor.matmul(S[64 * half:64 * half + 64, u, c * P:(c + 1) * P],
                                                        qs[64 * u:64 * u + 64, 4 * (r // 2) + c, 64 * half:64 * half + 64],
                                                        ks[64 * u:64 * u + 64, r // 2, 64 * half:64 * half + P], start=True, stop=True)
                        last.then_inc(sc_done, 1)

                    def transpose4(bank, src, done):
                        for c in range(4):
                            last = nc.tensor.transpose(bank[:, c * P:(c + 1) * P], src(c), C("ident"))
                        last.then_inc(done, 1)

                    def x_rows(r):
                        if r == 0:
                            pe.wait_ge(q_in, at(16, 16))
                            pe.wait_ge(k_in, at(16, 16))
                            pe.wait_ge(state_ready, at(4, 1))
                            pe.wait_ge(x2_in, at(16, 16))
                        if r < 2:
                            pe.wait_ge(yout_ready, at(4, 1 + r))
                        else:
                            pe.wait_ge(pT_ready, at(4, r + 1))
                        transpose4(Tb[:, r % 2, :], lambda c: xb[:, 4 * r + c, :], xr_done)

                    def probs_T(r):
                        pe.wait_ge(probs_ready, at(4, r + 1))
                        if r < 2:
                            pe.wait_ge(xdt_ready, at(4, r + 1))
                        else:
                            pe.wait_ge(pT_ready, at(4, r - 1))
                        transpose4(Tb[:, r % 2, :], lambda c: probs[:, r % 2, c, :], pt_done)

                    def attend(r):
                        pe.wait_ge(pT_ready, at(4, r + 1))
                        if r == 0:
                            pe.wait_ge(v_in, at(32, 32))
                            pe.wait_ge(yrow_ready, at(4, 1))
                        b = r // 2
                        for c in range(4):
                            to = (4 * (r % 2) + c) * HD
                            for half in range(2):
                                last = nc.tensor.matmul(O[64 * half:64 * half + 64, b, to:to + HD],
                                                        pT[:, r % 2, c, 64 * half:64 * half + 64],
                                                        vs[:, half, r * HD:(r + 1) * HD], start=True, stop=True)
                        if r % 2:
                            last.then_inc(pv_done, 1)

                    def o_T(b):
                        pe.wait_ge(orow_ready, at(2, b + 1))
                        pe.wait_ge(xdt_ready, at(4, 3 + b))
                        transpose4(Tb[:, b, :], lambda c: orow[:, b, c * P:(c + 1) * P], ot_done)

                    def b_rows_and_cb():
                        pe.wait_ge(bc_in, at(16, 16))
                        pe.wait_ge(probs_ready, at(4, 4))
                        transpose4(S[:, 0, :], lambda c: bc[:, c, :], brt_done)
                        for g in range(GROUPS):
                            last = nc.tensor.matmul(S[:, 1, g * P:(g + 1) * P], bc[:, g, :], bc[:, 4 + g, :], start=True, stop=True)
                        last.then_inc(cb_done, 1)

                    def group(g):
                        pe.wait_ge(wT_ready, at(4, g + 1))
                        if g == 0:
                            pe.wait_ge(orow_ready, at(2, 2))
                        else:
                            pe.wait_ge(yrow_ready, at(4, g + 1))
                        for h in range(HG):
                            nc.tensor.matmul(O[:, 0, h * HD:(h + 1) * HD], dec[:, g % 2, h, :], xdt[:, g, h * HD:(h + 1) * HD], start=True, stop=True)
                        nc.tensor.matmul(O[:, 1, :], bc[:, 4 + g, :], state[:, g, :], start=True, stop=True).then_inc(yg_done, 1)
                        pe.wait_ge(xdd_ready, at(4, g + 1))
                        if g == 0:
                            pe.wait_ge(brow_ready, at(1, 1))
                        elif g == 1:
                            pe.wait_ge(cbm_ready, at(1, 1))
                        else:
                            pe.wait_ge(state_ready, at(4, g))
                        nc.tensor.matmul(S[:, g % 2, :], brow[:, g, :], xdd[:, g, :], start=True, stop=True).then_inc(st_done, 1)

                    def y_T(g):
                        pe.wait_ge(yrow_ready, at(4, g + 2))
                        if g < 2:
                            pe.wait_ge(oT_ready, at(2, g + 1))
                        else:
                            pe.wait_ge(yout_ready, at(4, g + 1))
                        transpose4(Tb[:, g % 2, :], lambda c: yrow[:, g % 2, c * P:(c + 1) * P], yt_done)

                    def half_unit(h):
                        n = h // 2
                        if h % 2 == 0:
                            pe.wait_ge(w_hi, at(4, B2 + n + 1))
                            pe.wait_ge(w_lo, at(4, B2 + n + 1))
                        pe.wait_ge(half_taken, at(8, h + 1))
                        matmuls(F[:, h % 2, :], (B2 + n) % 2, X0, h % 2).then_inc(unit_done, 1)

                    x_rows(0)
                    x_rows(1)
                    scores(0)
                    scores(1)
                    half_unit(0)
                    probs_T(0)
                    probs_T(1)
                    scores(2)
                    scores(3)
                    half_unit(1)
                    attend(0)
                    attend(1)
                    probs_T(2)
                    probs_T(3)
                    half_unit(2)
                    attend(2)
                    attend(3)
                    x_rows(2)
                    x_rows(3)
                    b_rows_and_cb()
                    half_unit(3)
                    o_T(0)
                    o_T(1)
                    group(0)
                    half_unit(4)
                    y_T(0)
                    group(1)
                    half_unit(5)
                    y_T(1)
                    group(2)
                    half_unit(6)
                    y_T(2)
                    group(3)
                    half_unit(7)
                    y_T(3)

            @block.vector
            def _(dve):
                ch = Chain(dve, step2)
                dve.sem_inc(yout_ready, 2)
                dve.sem_inc(yrow_ready, 1)
                dve.sem_inc(seg_ready, 1)
                nc.vector.memset(state[:], 0.0).then_inc(state_ready, 1)
                ch.link(nc.vector.tensor_scalar(stat[:, 5, :], C("sinks"), -1.0, None, ALU.mult))
                for j in ch.loop(nc.vector.Fori, NT, 4 * 3 + 1 + 4):
                    def at(n, k):
                        return j * n + k

                    def per_head(ap, lo, n, width=HD):
                        return ap[:, ds(j, 1), lo:lo + n].rearrange("p a h -> p (a h)").unsqueeze(2).to_broadcast([P, n, width])

                    def maxima(r):
                        dve.wait_ge(sc_done, at(4, r + 2))
                        bank = S[:, r % 2, :].rearrange("p (c m) -> p c m", c=4)
                        ch.link(nc.vector.tensor_scalar(bank[0:CH, :, 0:CH], bank[0:CH, :, 0:CH],
                                                        C("pad_mask")[0:CH, ds(j, 1)], None, ALU.add))
                        h4 = slice(4 * r, 4 * r + 4)
                        ch.link(nc.vector.tensor_reduce(stat[:, 0, h4], bank, AX.X, ALU.max))
                        ch.link(nc.vector.scalar_tensor_tensor(stat[:, 1, h4], stat[:, 0, h4], -1.0,
                                                               rq_sb[:, ds(j, 1), h4].rearrange("p a h -> p (a h)"), ALU.mult, ALU.mult))
                        nc.vector.tensor_tensor(negm[:, h4], stat[:, 1, h4], stat[:, 5, h4], ALU.min).then_inc(negm_ready, 1)

                    def x_dt(r):
                        dve.wait_ge(xr_done, at(4, r + 2))
                        nc.vector.tensor_tensor(xdt[:, r, :].rearrange("p (h d) -> p h d", d=HD),
                                                Tb[:, r % 2, :].rearrange("p (h d) -> p h d", d=HD),
                                                per_head(dt_sb, 8 * r, 8), ALU.mult).then_inc(xdt_ready, 1)

                    def seg(g):
                        if g == 0:
                            dve.wait_ge(cs_in, at(16, 16))
                        if g >= 2:
                            dve.wait_ge(yg_done, at(4, g))
                        for h in range(HG):
                            last = nc.vector.tensor_scalar(dec[:, g % 2, h, :], csb[:, HG * g + h, :],
                                                           cs_sb[:, ds(j, 1), HG * g + h:HG * g + h + 1].rearrange("p a h -> p (a h)"),
                                                           0.0, ALU.subtract, ALU.min)
                        last.then_inc(seg_ready, 1)

                    def o_rows(b):
                        dve.wait_ge(pv_done, at(2, b + 2))
                        inv = stat[:, 4, 8 * b:8 * b + 8].unsqueeze(2).to_broadcast([P, 8, HD])
                        nc.vector.tensor_tensor(orow[:, b, :].rearrange("p (h d) -> p h d", d=HD),
                                                O[:, b, :].rearrange("p (h d) -> p h d", d=HD), inv, ALU.mult).then_inc(orow_ready, 1)

                    def o_out(b):
                        if b == 0:
                            dve.wait_ge(z_in, at(16, 16))
                        dve.wait_ge(ot_done, at(2, b + 1))
                        to = flat(zo[:, 4 * b:4 * b + 4, :])
                        nc.vector.tensor_tensor(to, to, Tb[:, b, :], ALU.mult).then_inc(oT_ready, 1)

                    def weights_T(g):
                        dve.wait_ge(dec_ready, at(4, g + 1))
                        nc.vector.tensor_tensor(dec[:, g % 2], dec[:, g % 2], cbm[:, g, :].unsqueeze(1).to_broadcast([P, HG, P]),
                                                ALU.mult).then_inc(wT_ready, 1)

                    def y_rows(g):
                        dve.wait_ge(yg_done, at(4, g + 2))
                        ch.link(nc.vector.tensor_tensor(ytmp[:].rearrange("p (h d) -> p h d", d=HD),
                                                        O[:, 1, :].rearrange("p (h d) -> p h d", d=HD),
                                                        per_head(ecs_sb, HG * g, HG), ALU.mult))
                        if g >= 2:
                            dve.wait_ge(yt_done, at(4, g - 1))
                        nc.vector.tensor_tensor(yrow[:, g % 2, :], O[:, 0, :], ytmp[:], ALU.add).then_inc(yrow_ready, 1)

                    def add_state(g):
                        dve.wait_ge(st_done, at(4, g + 1))
                        dve.wait_ge(sdec_ready, at(4, g + 1))
                        nc.vector.tensor_tensor(state[:, g, :], state[:, g, :], S[:, g % 2, :], ALU.add).then_inc(state_ready, 1)

                    def y_out(g):
                        dve.wait_ge(yt_done, at(4, g + 1))
                        if g == 0:
                            dve.wait_ge(xd_ready, at(4, 5))
                        to = flat(yo[:, 4 * g:4 * g + 4, :])
                        nc.vector.tensor_tensor(to, to, Tb[:, g % 2, :], ALU.add).then_inc(yout_ready, 1)

                    maxima(0)
                    maxima(1)
                    x_dt(0)
                    x_dt(1)
                    maxima(2)
                    maxima(3)
                    dve.wait_ge(negm_ready, at(4, 4))
                    nc.vector.tensor_tensor(stat[:, 3, :], C("sinks"), negm[:], ALU.add).then_inc(sinkm_ready, 1)
                    seg(0)
                    seg(1)
                    dve.wait_ge(sinke_ready, at(1, 1))
                    ch.link(nc.vector.tensor_tensor(stat[:, 3, :], stat[:, 3, :], stat[:, 2, :], ALU.add))
                    nc.vector.reciprocal(stat[:, 4, :], stat[:, 3, :]).then_inc(rsum_ready, 1)
                    dve.wait_ge(rsum_ready, at(1, 1))
                    o_rows(0)
                    o_rows(1)
                    x_dt(2)
                    x_dt(3)
                    dve.wait_ge(cb_done, at(1, 1))
                    nc.vector.tensor_tensor(cbm[:], S[:, 1, :].rearrange("p (g l) -> p g l", g=GROUPS),
                                            C("tri").unsqueeze(1).to_broadcast([P, GROUPS, P]), ALU.mult).then_inc(cbm_ready, 1)
                    dve.wait_ge(cbm_ready, at(1, 1))
                    weights_T(0)
                    weights_T(1)
                    o_out(0)
                    o_out(1)
                    for g in range(GROUPS):
                        y_rows(g)
                        if g + 2 < GROUPS:
                            seg(g + 2)
                        add_state(g)
                        if g >= 1:
                            y_out(g - 1)
                        if g + 2 < GROUPS:
                            weights_T(g + 2)
                    y_out(3)

            @block.scalar
            def _(act):
                act.sem_inc(half_taken, 2)
                act.sem_inc(o_stored, 16)
                for p in range(2):
                    act.sem_inc(f_stored[p], 16)
                with nc.scalar.Fori(0, NT) as j:
                    def at(n, k):
                        return j * n + k

                    def exps(r):
                        act.wait_ge(negm_ready, at(4, r + 1))
                        for c in range(4):
                            h = 4 * r + c
                            last = nc.scalar.activation(probs[:, r % 2, c, :], S[:, r % 2, c * P:(c + 1) * P], ACT.Exp,
                                                        bias=negm[:, h:h + 1], scale=rq_sb[:, ds(j, 1), h:h + 1].rearrange("p a h -> p (a h)"),
                                                        accum_out=stat[:, 2, h:h + 1])
                        last.then_inc(probs_ready, 1)

                    def probs_out(r):
                        act.wait_ge(pt_done, at(4, r + 1))
                        if r >= 2:
                            act.wait_ge(pv_done, at(2, 2))
                        nc.scalar.activation(flat(pT[:, r % 2]), Tb[:, r % 2, :], ACT.Copy).then_inc(pT_ready, 1)

                    def decay(g):
                        act.wait_ge(seg_ready, at(4, g + 2))
                        nc.scalar.activation(dec[:, g % 2], dec[:, g % 2], ACT.Exp).then_inc(dec_ready, 1)

                    def take_half(h):
                        n, p = h // 2, (h // 2) % 2
                        act.wait_ge(unit_done, at(8, 2 * B2 + h + 1))
                        if h % 2 == 0:
                            act.wait_ge(f_stored[p], at(32, 16 * (n // 2) + 16))
                        nc.scalar.activation(fres[:, p, (h % 2) * HALF:(h % 2 + 1) * HALF], F[:, h % 2, :], ACT.Copy).then_inc(half_taken, 1)
                        if h % 2:
                            high(act, B2 + n + 2, 4, j)
                            act.wait_ge(half_taken, at(8, h + 3))
                            to = z_d[ds(j * 2 + (8 + n), 1)] if n < 2 else g_d[ds(j * 2 + (n - 2), 1)]
                            act.dma_start(to, fres[:, p, :]).then_inc(f_stored[p], 16)

                    exps(0)
                    exps(1)
                    take_half(0)
                    probs_out(0)
                    probs_out(1)
                    exps(2)
                    exps(3)
                    act.wait_ge(sinkm_ready, at(1, 1))
                    nc.scalar.activation(stat[:, 3, :], stat[:, 3, :], ACT.Exp).then_inc(sinke_ready, 1)
                    take_half(1)
                    probs_out(2)
                    probs_out(3)
                    decay(0)
                    decay(1)
                    take_half(2)
                    act.wait_ge(brt_done, at(1, 1))
                    nc.scalar.activation(flat(brow[:]), S[:, 0, :], ACT.Copy).then_inc(brow_ready, 1)
                    take_half(3)
                    take_half(4)
                    act.wait_ge(oT_ready, at(2, 2))
                    act.dma_start(o_d[:, :, ds(j * P, P)].rearrange("n p t -> p n t"), zo[:]).then_inc(o_stored, 16)
                    decay(2)
                    take_half(5)
                    decay(3)
                    take_half(6)
                    take_half(7)
                act.wait_ge(o_stored, 16 * (NT + 1))
                for p in range(2):
                    act.wait_ge(f_stored[p], 16 * (2 * NT + 1))

            @block.gpsimd
            def _(pool):
                pool.sem_inc(xd_ready, 1)
                with nc.gpsimd.Fori(0, NT) as j:
                    def at(n, k):
                        return j * n + k

                    def per_head(ap, lo, n):
                        return ap[:, ds(j, 1), lo:lo + n].rearrange("p a h -> p (a h)").unsqueeze(2).to_broadcast([P, n, HD])

                    def x_dd(g):
                        pool.wait_ge(xdt_ready, at(4, g + 1))
                        nc.gpsimd.tensor_tensor(xdd[:, g, :].rearrange("p (h d) -> p h d", d=HD),
                                                xdt[:, g, :].rearrange("p (h d) -> p h d", d=HD),
                                                per_head(de_sb, HG * g, HG), ALU.mult).then_inc(xdd_ready, 1)

                    def decay_state(g):
                        pool.wait_ge(yg_done, at(4, g + 2))
                        to = state[:, g, :].rearrange("p (h d) -> p h d", d=HD)
                        nc.gpsimd.tensor_tensor(to, to, per_head(cd_sb, HG * g, HG), ALU.mult).then_inc(sdec_ready, 1)

                    pool.wait_ge(x2_in, at(16, 16))
                    nc.gpsimd.tensor_tensor(yo[:], xb[:], C("d_skip").unsqueeze(2).to_broadcast([P, 16, P]), ALU.mult).then_inc(xd_ready, 4)
                    x_dd(0)
                    x_dd(1)
                    low(pool, B2 + 0 + 2, 4, j)
                    x_dd(2)
                    x_dd(3)
                    low(pool, B2 + 1 + 2, 4, j)
                    decay_state(0)
                    decay_state(1)
                    low(pool, B2 + 2 + 2, 4, j)
                    decay_state(2)
                    decay_state(3)
                    low(pool, B2 + 3 + 2, 4, j)
                    pool.wait_ge(yout_ready, at(4, 6))
                    pool.dma_start(y_d[:, :, ds(j * P, P)].rearrange("n p t -> p n t"), yo[:]).then_inc(y_stored, 16)
                    pool.wait_ge(y_stored, at(16, 16))

        with ExitStack() as ctx:
            X1 = sbuf(ctx, "X1", [P, 2, NK, T], f32r)
            acc = sbuf(ctx, "acc", [P, NK, T])
            part = sbuf(ctx, "part", [P, 2, T])
            gate = sbuf(ctx, "gate", [P, 2, T])
            ms = ssd_sb[:, 0:4].rearrange("p n t h -> p (n t h)")
            F = ctx.enter_context(nc.psum_tensor("F3", [P, 4, 512], f32))
            M = ctx.enter_context(nc.psum_tensor("M3", [P, 4, 512], f32))
            (step3, silu3, gated, y_sq, sq_done, act_hi, act_lo, gateA_ready, gateB_ready, gr_ready, ms_done, ms_rt, rms_ready,
             acc_ready, m_hi, m_lo, rows_in, row_done, out_ready, out_stored) = sems(
                ctx, "step3", "silu3", "gated", "y_sq", "sq_done", "act_hi", "act_lo", "gateA_ready", "gateB_ready", "gr_ready",
                "ms_done", "ms_rt", "rms_ready", "acc_ready", "m_hi", "m_lo", "rows_in", "row_done", "out_ready", "out_stored")
            o_in = sems(ctx, *[f"o_in{k}" for k in range(NK)])
            gateA_in = sems(ctx, "gateA_in0", "gateA_in1")
            y_in = sems(ctx, "y_in0", "y_in1")
            merge_in = sems(ctx, "merge_in0", "merge_in1")
            a_stored = sems(ctx, "a_stored0", "a_stored1")
            pair3_free = sems(ctx, "pair3_free0", "pair3_free1")

            def pair3(p):
                return F[:, 2 * p:2 * p + 2, :].rearrange("p b c -> p (b c)")

            def row_bank(t):
                return M[:, t, :] if t < 4 else F[:, t - 4, :]

            def tile(X, part, i, s=0):
                return X[:, part, ds(i * 2 + s, 1), :].rearrange("p a t -> p (a t)").bitcast(f32)

            def split_tile(X, part, i, s):
                return X[:, part, ds(i * 2 + s, 1), :].rearrange("p a t -> p (a t)")

            def column(name, i, s):
                return C(name)[:, ds(i * 2 + s, 1)]

            def acc_tile(i, s):
                return acc[:, ds(i * 2 + s, 1), :].rearrange("p a t -> p (a t)")

            def row(ap):
                return ap.rearrange("a p t -> (a p) t")

            block = ctx.enter_context(nc.Block())

            @block.sync
            def _(sp):
                def load_gateA(i, s):
                    sp.dma_start(acc_tile(i, s), row(g_d[ds(i * 2 + s, 1)])).then_inc(gateA_in[s], 16)

                def load_y(X, q0, i, s):
                    sp.dma_start(tile(X, 1, i, s), row(y_d[ds(i * 2 + (q0 + s), 1)])).then_inc(y_in[s], 16)
                    sp.dma_start(tile(X, 0, i, s), row(z_d[ds(i * 2 + (8 + q0 + s), 1)])).then_inc(y_in[s], 16)

                def load_merge(i, s):
                    sp.dma_start(gate[:, s, :], row(g_d[ds(i * 2 + (8 + s), 1)])).then_inc(merge_in[s], 16)
                    sp.dma_start(part[:, s, :], row(a_d[ds(i * 2 + s, 1)])).then_inc(merge_in[s], 16)

                for s in range(2):
                    sp.sem_inc(a_stored[s], 16)
                for k in range(NK):
                    sp.dma_start(X1[:, 1, k, :].bitcast(f32), o_d[k]).then_inc(o_in[k], 16)
                for s in range(2):
                    load_gateA(0, s)
                    load_y(X0, 0, 0, s)
                with nc.sync.Fori(0, 3) as i:
                    for s in range(2):
                        load_w(sp, B3 + 2 + s, 2, i)
                        sp.wait_ge(gateA_ready, i * 2 + (s + 1))
                        load_gateA(i + 1, s)
                        sp.wait_ge(act_lo, i * 2 + (NK + s + 1))
                        load_y(X0, 0, i + 1, s)
                for s in range(2):
                    load_w(sp, B3 + 8 + s, 0, 0)
                for s in range(2):
                    sp.wait_ge(unit_done, 2 * (B3 + 8))
                    sp.wait_ge(act_lo, NK + 7 + s)
                    load_y(X1, 8, 0, s)

                def pass1_turn(i, s):
                    load_w(sp, B3 + 10 + s, 2, i)
                    sp.wait_ge(pair3_free[s], i * 2 + 2)
                    sp.wait_ge(a_stored[s], i * 16 + 16)
                    sp.dma_start(row(a_d[ds(i * 2 + s, 1)]), acc_tile(i, s)).then_inc(a_stored[s], 16)

                with nc.sync.Fori(0, 3) as i:
                    for s in range(2):
                        pass1_turn(i, s)
                        sp.wait_ge(act_lo, i * 2 + (NK + 9 + s))
                        load_y(X1, 8, i + 1, s)
                for s in range(2):
                    pass1_turn(3, s)
                sp.wait_ge(sq_done, 16)
                for s in range(2):
                    load_merge(0, s)

                def load_rows(i, s):
                    sp.dma_start(acc_tile(i, s), a["x"][ds(i * (2 * P) + s * P, P), :]).then_inc(rows_in, 16)

                with nc.sync.Fori(0, 3) as i:
                    for s in range(2):
                        load_w(sp, B3 + 18 + s, 2, i)
                        sp.wait_ge(m_lo, i * 4 + (2 * s + 2))
                        load_merge(i + 1, s)
                        load_rows(i, s)
                for s in range(2):
                    load_w(sp, B3 + 24 + s, 0, 0)
                for s in range(2):
                    sp.wait_ge(m_lo, 14 + 2 * s)
                    load_rows(3, s)
                with nc.sync.Fori(0, 3) as i:
                    for s in range(2):
                        load_w(sp, B3 + 26 + s, 2, i)
                for c in range(2):
                    for t in range(NT):
                        sp.wait_ge(out_ready, 8 + NT * c + t + 1)
                        to = slice(c * HALF, (c + 1) * HALF)
                        sp.dma_start(out[t * P:(t + 1) * P, to], acc[:, t, to]).then_inc(out_stored, 16)
                sp.wait_ge(out_stored, 16 * 2 * NT)

            @block.gpsimd
            def _(pool):
                ch = Chain(pool, sq_done)
                nc.gpsimd.memset(ms, 0.0).then_inc(y_sq, 1)

                def squares(X, k0, i, s):
                    pool.wait_ge(gated, i * 2 + (k0 + s + 1))
                    nc.gpsimd.tensor_tensor(part[:, s, :], tile(X, 1, i, s), tile(X, 1, i, s), ALU.mult).then_inc(y_sq, 1)
                    pool.wait_ge(y_sq, i * 2 + (k0 + s + 2))
                    ch.link(nc.gpsimd.tensor_tensor(ms, ms, part[:, s, :], ALU.add))

                for n0, X in ((0, X0), (8, X1)):
                    for i in ch.loop(nc.gpsimd.Fori, 4, 2):
                        for s in range(2):
                            squares(X, n0, i, s)
                            low(pool, B3 + n0 + 2 + s, 2, i)
                pool.wait_ge(rms_ready, 1)
                with nc.gpsimd.Fori(0, 4) as i:
                    for s in range(2):
                        pool.wait_ge(gateB_ready, i * 2 + (s + 1))
                        nc.gpsimd.tensor_tensor(gate[:, s, :], gate[:, s, :], ms, ALU.mult).then_inc(gr_ready, 1)
                        low(pool, B3 + 18 + s, 2, i)
                with nc.gpsimd.Fori(0, 3) as i:
                    for s in range(2):
                        low(pool, B3 + 26 + s, 2, i)

            @block.scalar
            def _(act):
                def silu_and_high(X, q0, i, s):
                    act.wait_ge(y_in[s], i * 32 + (16 * q0 + 32))
                    nc.scalar.activation(tile(X, 0, i, s), tile(X, 0, i, s), ACT.Silu).then_inc(silu3, 1)
                    act.wait_ge(gated, i * 2 + (q0 + s + 1))
                    nc.scalar.activation(split_tile(X, 0, i, s), tile(X, 1, i, s), ACT.Identity,
                                         scale=C("ssd_gain", q0, q0 + 8)[:, ds(i * 2 + s, 1)]).then_inc(act_hi, 1)

                for k in range(NK):
                    act.wait_ge(o_in[k], 16)
                    nc.scalar.activation(X1[:, 0, k, :], X1[:, 1, k, :].bitcast(f32), ACT.Copy).then_inc(act_hi, 1)
                with nc.scalar.Fori(0, 4) as i:
                    for s in range(2):
                        act.wait_ge(gateA_in[s], i * 16 + 16)
                        nc.scalar.activation(acc_tile(i, s), acc_tile(i, s), ACT.Sigmoid,
                                             bias=C("b_gate", 0, 8)[:, ds(i * 2 + s, 1)]).then_inc(gateA_ready, 1)
                        silu_and_high(X0, 0, i, s)
                        high(act, B3 + 2 + s, 2, i)
                with nc.scalar.Fori(0, 4) as i:
                    for s in range(2):
                        silu_and_high(X1, 8, i, s)
                        high(act, B3 + 10 + s, 2, i)
                        act.wait_ge(a_stored[s], i * 16 + 32)
                        nc.scalar.activation(acc_tile(i, s), pair3(s), ACT.Copy).then_inc(pair3_free[s], 2)
                act.wait_ge(ms_done, 1)
                nc.scalar.activation(ms, flat(M[:, 0:2, :]), ACT.Sqrt, bias=eps[:], scale=1.0 / (2 * DM)).then_inc(ms_rt, 1)

                def merged_high(i, s, h):
                    act.wait_ge(acc_ready, i * 4 + (2 * s + h + 1))
                    to = slice(h * HALF, (h + 1) * HALF)
                    nc.scalar.activation(split_tile(X0, 0, i, s)[:, to], acc_tile(i, s)[:, to], ACT.Copy).then_inc(m_hi, 1)

                with nc.scalar.Fori(0, 4) as i:
                    for s in range(2):
                        act.wait_ge(merge_in[s], i * 32 + 32)
                        nc.scalar.activation(gate[:, s, :], gate[:, s, :], ACT.Sigmoid,
                                             bias=C("b_gate", 8, 16)[:, ds(i * 2 + s, 1)]).then_inc(gateB_ready, 1)
                        merged_high(i, s, 0)
                        high(act, B3 + 18 + s, 2, i)
                        merged_high(i, s, 1)
                with nc.scalar.Fori(0, 3) as i:
                    for s in range(2):
                        high(act, B3 + 26 + s, 2, i)

            @block.vector
            def _(dve):
                ch = Chain(dve, step3)

                def gate_and_low(X, q0, i, s):
                    y, n = tile(X, 1, i, s), q0 + s + 1
                    dve.wait_ge(silu3, i * 2 + n)
                    nc.vector.tensor_tensor(y, y, tile(X, 0, i, s), ALU.mult).then_inc(gated, 1)
                    dve.wait_ge(act_hi, i * 2 + (NK + n))
                    dve.wait_ge(y_sq, i * 2 + (n + 1))
                    nc.vector.scalar_tensor_tensor(split_tile(X, 1, i, s), y, C("ssd_gain", q0, q0 + 8)[:, ds(i * 2 + s, 1)],
                                                   tile(X, 0, i, s), ALU.mult, ALU.subtract).then_inc(act_lo, 1)

                for k in range(NK):
                    dve.wait_ge(act_hi, k + 1)
                    nc.vector.tensor_tensor(X1[:, 1, k, :], X1[:, 1, k, :].bitcast(f32), X1[:, 0, k, :].bitcast(f32),
                                            ALU.subtract).then_inc(act_lo, 1)
                with nc.vector.Fori(0, 4) as i:
                    for s in range(2):
                        gate_and_low(X0, 0, i, s)
                        dve.wait_ge(gateA_ready, i * 2 + (s + 1))
                        dve.wait_ge(unit_done, i * 4 + 2 * (B3 + s + 1))
                        nc.vector.tensor_tensor(acc_tile(i, s), acc_tile(i, s), pair3(s), ALU.mult).then_inc(pair3_free[s], 2)
                with nc.vector.Fori(0, 4) as i:
                    for s in range(2):
                        gate_and_low(X1, 8, i, s)
                dve.wait_ge(ms_rt, 1)
                nc.vector.reciprocal(ms, ms).then_inc(rms_ready, 1)
                for i in ch.loop(nc.vector.Fori, 4, 8):
                    for s in range(2):
                        for h in range(2):
                            to = slice(h * HALF, (h + 1) * HALF)
                            sum_b = acc_tile(i, s)[:, to]
                            dve.wait_ge(unit_done, i * 4 + (2 * (B3 + 16 + s) + h + 1))
                            ch.link(nc.vector.tensor_tensor(sum_b, sum_b, F[:, 2 * s + h, :], ALU.add))
                            dve.sem_inc(pair3_free[s], 1)
                            dve.wait_ge(gr_ready, i * 2 + (s + 1))
                            ch.link(nc.vector.tensor_tensor(sum_b, sum_b, gate[:, s, to], ALU.mult))
                            dve.wait_ge(merge_in[s], i * 32 + 32)
                            nc.vector.tensor_tensor(sum_b, sum_b, part[:, s, to], ALU.add).then_inc(acc_ready, 1)
                            dve.wait_ge(m_hi, i * 4 + (2 * s + h + 1))
                            nc.vector.tensor_tensor(split_tile(X0, 1, i, s)[:, to], sum_b, tile(X0, 0, i, s)[:, to],
                                                    ALU.subtract).then_inc(m_lo, 1)
                dve.wait_ge(rows_in, 16 * NT)
                for c in range(2):
                    for t in range(NT):
                        if t < NT - 1:
                            dve.wait_ge(row_done, (NT - 1) * c + t + 1)
                        else:
                            dve.wait_ge(unit_done, 2 * (B3 + 28 + 4 * c))
                        to = acc[:, t, c * HALF:(c + 1) * HALF]
                        nc.vector.tensor_tensor(to, to, row_bank(t), ALU.add).then_inc(out_ready, 1)

            @block.tensor
            def _(pe):
                pe.sem_inc(out_ready, 8)

                def unit3(n, act, i, free=True, by_tile=False):
                    s = n % 2
                    pe.wait_ge(w_hi, i * 2 + (B3 + n + 1))
                    pe.wait_ge(w_lo, i * 2 + (B3 + n + 1))
                    if free:
                        pe.wait_ge(pair3_free[s], i * 2 + 2 * (n // 2))
                    for h in range(2):
                        if by_tile and h == 0:
                            for k in range(NK):
                                pe.wait_ge(act_lo, k + 1)
                                for wp, ap in ((0, 0), (0, 1), (1, 0)):
                                    last = nc.tensor.matmul(F[:, 2 * s, :], whl[:, 1 - s, wp, k, :], act[:, ap, k, 0:HALF],
                                                            start=(k == 0 and wp == 0 and ap == 0), stop=(k == NK - 1 and wp == 1))
                            last.then_inc(unit_done, 1)
                        else:
                            matmuls(F[:, 2 * s + h, :], 1 - s, act, h).then_inc(unit_done, 1)

                unit3(0, X1, 0, free=False, by_tile=True)
                unit3(1, X1, 0, free=False)
                with nc.tensor.Fori(0, 3) as i:
                    for s in range(2):
                        unit3(2 + s, X1, i)
                pe.wait_ge(act_lo, 16)
                with nc.tensor.Fori(0, 4) as i:
                    for s in range(2):
                        unit3(8 + s, X0, i)
                pe.wait_ge(act_lo, 24)
                pe.wait_ge(sq_done, 16)
                for h in range(2):
                    last = nc.tensor.matmul(M[:, h, :], C("ones"), ms[:, h * HALF:(h + 1) * HALF], start=True, stop=True)
                last.then_inc(ms_done, 1)
                for n in (16, 17):
                    unit3(n, X1, 0)
                with nc.tensor.Fori(0, 3) as i:
                    for s in range(2):
                        unit3(18 + s, X1, i)
                with nc.tensor.Fori(0, 2) as c:
                    for kp in range(4):
                        n = 24 + kp
                        slot = (n + 1) % 2
                        pe.wait_ge(w_hi, c * 4 + (B3 + n + 1))
                        pe.wait_ge(w_lo, c * 4 + (B3 + n + 1))
                        w_half = whl[:, slot].rearrange("p w k c -> p w (k c)")
                        for t0, k in ((0, 2 * kp), (0, 2 * kp + 1), (4, 2 * kp), (4, 2 * kp + 1)):
                            pe.wait_ge(m_lo, 2 * k + 2)
                            if k == 0 and t0 == 4:
                                for p in range(2):
                                    pe.wait_ge(pair3_free[p], 24)
                            for t in range(t0, t0 + 4):
                                if k == 0:
                                    pe.wait_ge(out_ready, c * 8 + (t + 1))
                                for wp, ap in ((0, 0), (1, 0), (0, 1)):
                                    last = nc.tensor.matmul(row_bank(t), X0[:, ap, k, t * P:(t + 1) * P],
                                                            w_half[:, wp, (k % 2) * HALF:(k % 2 + 1) * HALF],
                                                            start=(k == 0 and wp == 0 and ap == 0), stop=(k == NK - 1 and ap == 1))
                                if k == NK - 1 and t < NT - 1:
                                    last.then_inc(row_done, 1)
                        last.then_inc(unit_done, 2)


def kernel(**inputs):
    import numpy as np
    import concourse.bacc as bacc
    from concourse.bass_utils import run_bass_kernel_spmd

    def cols(v):
        return np.ascontiguousarray(v.reshape(-1, P).T)

    def rows(v):
        return np.broadcast_to(v, (P, v.size))

    w = {n: np.ascontiguousarray(v[0], dtype=np.float32) for n, v in inputs.items()}
    s = np.arange(P)
    parts = {
        "conv_w": w["conv_w"].reshape(4, NX, P).transpose(2, 1, 0).reshape(P, NX * 4),
        "conv_b": cols(w["conv_b"]), "b_gate": cols(w["b_gate"]), "ssd_gain": cols(w["ssd_norm_gain"]),
        "d_skip": cols(np.repeat(w["d_skip"], HD)),
        "q_gain": cols(np.tile(w["q_norm_gain"], 2)), "k_gain": cols(np.tile(w["k_norm_gain"], 2)),
        "dt_bias": rows(w["dt_bias"]), "a_log": rows(w["a_log"]),
        "sinks": rows(w["attn_sinks"]),
        "pad_mask": np.where(np.arange(NT)[None, :] == 0, NEG, 0.0) * (s[:, None] < CH),
        "ident": np.eye(P), "tri": s[:, None] <= s[None, :],
        "ones": np.ones((P, P)), "head_ones": s[:, None] // HD == s[None, :] // HD, "head_sel": s[:, None] // HD == np.arange(2)[None, :],
    }
    consts = np.concatenate([np.asarray(parts[n], np.float32) for n, _ in CONST_COLS], axis=1)
    half = HD // 2
    inv = np.float32(10000.0) ** (-np.arange(half, dtype=np.float32) / half)
    ang = np.arange(T, dtype=np.float32)[None, :] * inv[:, None]
    cos = np.tile(np.cos(ang), (4, 1)).astype(np.float32)
    sin = np.tile(np.concatenate([np.sin(ang), -np.sin(ang)]), (2, 1)).astype(np.float32)

    def units(m):
        return m.reshape(NK, P, -1, P).transpose(2, 1, 0, 3).reshape(-1, P, NK * P)

    def row_units(m):
        return m.reshape(NK // 2, 2, P, 2, HALF).transpose(3, 0, 2, 1, 4).reshape(-1, P, NK * P)

    q, k, v, z_a, z_s, xbc, dt, g = np.split(w["w_in"], np.cumsum([1024, 256, 256, 1024, 2048, NX * P, NHS]), axis=1)
    q = q.reshape(DM, 2, 2, 4, HD).transpose(0, 1, 3, 2, 4).reshape(DM, DM)
    dt = np.concatenate([dt, np.zeros((DM, P - NHS), np.float32)], axis=1)
    per_tile = np.concatenate([units(z_s).reshape(NT, 2, P, -1), units(g).reshape(NT, 2, P, -1)], axis=1)
    w_units = np.concatenate([units(dt), units(v), units(k), units(q), units(xbc), units(z_a), per_tile.reshape(4 * NT, P, -1),
                              units(w["w_attn_proj"]), units(w["w_ssd_proj"][:DM]), units(w["w_ssd_proj"][DM:]), row_units(w["w_out"])])
    assert len(w_units) == UNITS
    arrays = {"x": w["x"], "w_units": w_units, "consts": consts, "gain": np.ascontiguousarray(rows(w["norm_gain"])),
              "cos": cos, "sin": sin}
    nc = bacc.Bacc("TRN2", target_bir_lowering=False, num_devices=1)
    aps = {n: nc.dram_tensor(n, v.shape, mybir.dt.float32, kind="ExternalInput").ap() for n, v in arrays.items()}
    out = nc.dram_tensor("out", (T, DM), mybir.dt.float32, kind="ExternalOutput").ap()
    build(nc, aps, out)
    r = run_bass_kernel_spmd(nc, [arrays], core_ids=[0])
    return r.results[0]["out"].reshape(1, T, DM)
```

```python
import concourse.bass as bass
from concourse import mybir
from contextlib import ExitStack
import numpy as np

P = 128
T = 1024
DM = 1024
NT = T // P
NK = DM // P
HALF = T // 2
CH = 64
HD = 64
NH = 16
NKV = 4
GROUPS = 4
HG = 8
NHS = GROUPS * HG
V0, K0, Q0, X0U, Z0 = 1, 3, 5, 13, 37
B2, B3, UNITS = 45, 77, 109
NX = 24
EPS = 1e-6
NEG = -1e30

CONST_COLS = [("b_gate", 16), ("ssd_gain", 16), ("d_skip", 16), ("sinks", NH), ("pad_mask", NT), ("ident", P), ("tri", P),
              ("ones", P), ("conv_w", NX * 4), ("conv_b", NX), ("q_gain", 1), ("k_gain", 1), ("dt_bias", NHS),
              ("a_log", NHS), ("head_ones", P), ("head_sel", 2)]
CONST_AT = {}
_at = 0
for _n, _w in CONST_COLS:
    CONST_AT[_n] = (_at, _at + _w)
    _at += _w
NCONST = _at
PART1_CONSTS = CONST_AT["conv_w"][0]


class Chain:

    def __init__(self, eng, sem):
        self.eng, self.sem, self.n = eng, sem, 0

    def link(self, ins):
        ins.then_inc(self.sem, 1)
        self.n = self.n + 1
        self.eng.wait_ge(self.sem, self.n)

    def loop(self, eng_loop, count, steps):
        base = self.n
        with eng_loop(0, count) as i:
            self.n = i * steps + base
            self.k = 0
            yield i
        self.n = base + count * steps


def build(nc, a, out):
    f32, f32r = mybir.dt.float32, mybir.dt.float32r
    ALU, ACT, AX = mybir.AluOpType, mybir.ActivationFunctionType, mybir.AxisListType
    ds = bass.ds

    def dram(name, shape):
        return nc.dram_tensor(name, shape, f32, kind="Internal").ap()

    q_d = dram("q_d", (8, P, T))
    k_d = dram("k_d", (2, P, CH + T))
    v_d = dram("v_d", (CH + T, NKV * HD))
    x_d = dram("x_d", (NX, P, T))
    z_d = dram("z_d", (24, P, T))
    g_d = dram("g_d", (16, P, T))
    cs_d = dram("cs_d", (NHS, T))
    ecs_d = dram("ecs_d", (NHS, T))
    o_d = dram("o_d", (8, P, T))
    y_d = dram("y_d", (16, P, T))
    a_d = dram("a_d", (8, P, T))

    root = ExitStack()
    with root:
        def sbuf(name, shape, dt=f32):
            return root.enter_context(nc.sbuf_tensor("sb_" + name, shape, dt))

        def sems(*names):
            return [root.enter_context(nc.semaphore(n)) for n in names]

        cst = sbuf("cst", [P, PART1_CONSTS])
        const_tiles = [(0, cst)]

        def C(name, lo=0, hi=None):
            b, e = CONST_AT[name]
            first, tile = const_tiles[b >= PART1_CONSTS]
            return tile[:, b - first + lo:(e if hi is None else b + hi) - first]

        wst = sbuf("wst", [P, 2, NK, P])
        whl = sbuf("whl", [P, 2, 2, NK, P], f32r)
        ssd_sb = sbuf("ssd_sb", [P, 4, NT, NHS])
        dt_sb = ssd_sb[:, 0]
        cs_sb = ssd_sb[:, 1]
        cd_sb = ssd_sb[:, 2]
        de_sb = ssd_sb[:, 3]
        rq_sb = sbuf("rq_sb", [P, NT, NH])
        eps = sbuf("eps", [P, 1])
        X0 = sbuf("X0", [P, 2, NK, T], f32r)
        with nc.sbuf_tensor("sb_early", [P, 2, NK * T], f32) as early:
            X1_high, X1_low = early[:, 0], early[:, 1]
        X1 = sbuf("X1", [P, 2, NK, T], f32r)
        acc = sbuf("acc", [P, NK, T])
        part = sbuf("part", [P, 2, T])
        res = sbuf("res", [P, 2, T])
        F = root.enter_context(nc.psum_tensor("F", [P, 4, 512], f32))
        M = root.enter_context(nc.psum_tensor("M", [P, 4, 512], f32))
        acc_all = acc[:, :, :].rearrange("p k t -> p (k t)")

        def carve(region, at, *shape):
            end = at + int(np.prod(shape))
            view = region[:, at:end]
            if len(shape) == 2:
                view = view.rearrange("p (a b) -> p a b", b=shape[1])
            elif len(shape) == 3:
                view = view.rearrange("p (a b c) -> p a b c", b=shape[1], c=shape[2])
            return view, end

        def flat(ap):
            return ap.rearrange("p a b -> p (a b)")

        def matmuls(bank, slot, act, half):
            for k in range(NK):
                for wp, ap in ((0, 0), (0, 1), (1, 0)):
                    last = nc.tensor.matmul(bank, whl[:, slot, wp, k, :],
                                            act[:, ap, k, half * HALF:(half + 1) * HALF],
                                            start=(k == 0 and wp == 0 and ap == 0),
                                            stop=(k == NK - 1 and wp == 1))
            return last

        def split_high(slot):
            return nc.scalar.activation(whl[:, slot, 0], wst[:, slot], ACT.Copy)

        def split_low(slot):
            return nc.gpsimd.tensor_tensor(whl[:, slot, 1], wst[:, slot], whl[:, slot, 0].bitcast(f32), ALU.subtract)

        w_in = sems("w_in0", "w_in1")
        w_hi, w_lo, unit_done = sems("w_hi", "w_lo", "unit_done")

        def load_w(sp, u, c, at):
            if u >= 2:
                sp.wait_ge(w_hi, at * c + (u - 1))
                sp.wait_ge(w_lo, at * c + (u - 1))
            src = a["w_units"][ds(at * c + u, 1)] if c else a["w_units"][u:u + 1]
            sp.dma_start(wst[:, u % 2].rearrange("p k c -> p (k c)"), src.rearrange("a p c -> (a p) c")).then_inc(w_in[u % 2], 16)

        def high(act, u, c, at):
            act.wait_ge(w_in[u % 2], at * (8 * c) + 16 * (u // 2 + 1))
            if u >= 2:
                act.wait_ge(unit_done, at * (2 * c) + 2 * (u - 1))
            split_high(u % 2).then_inc(w_hi, 1)

        def low(pool, u, c, at):
            pool.wait_ge(w_hi, at * c + (u + 1))
            split_low(u % 2).then_inc(w_lo, 1)

        block = root.enter_context(nc.Block())

        xrow, _ = carve(X1_high, 0, NT, DM)
        staged = xrow
        krms = xrow[:, 3:5, :]
        ecsT = xrow[0:NHS, 5, :]
        gain, w = carve(X1_low, 0, DM)
        cos, w = carve(X1_low, w, T)
        sin, w = carve(X1_low, w, T)
        cv, w = carve(X1_low, w, 2, T)
        gq, w = carve(X1_low, w, 2, T)
        csT, w = carve(X1_low, w, T)
        csT = csT[0:NHS, :]
        sq, w = carve(acc_all, 0, 2, T)
        small, w = carve(acc_all, w, 6, NT, NHS)
        cst1, w = carve(acc_all, w, NCONST - PART1_CONSTS)
        const_tiles.append((PART1_CONSTS, cst1))
        ssx, w = carve(acc_all, w, 2, NT)
        neg_a, w = carve(acc_all, w, NHS)
        zpad, w = carve(acc_all, w, 256)
        (consts_in, gain_in, rope_in, x_sq, x_rt, xn_ready, xt_done, x_hi, x_lo, dve_step, dtT_done,
         dt_z, dt_e, dt_w, dt_l, dA_ready, cs_done, cs_a, vT_done, v_ready, pads_set, pads_in,
         csT_done, csT_ready, cs_stored, gq_ready, rope_done, kss_done, k_rt, ssq_done, conv_done, silu_done,
         qst_rt, z_taken, gq_free) = sems(
            "consts_in", "gain_in", "rope_in", "x_sq", "x_rt", "xn_ready", "xt_done", "x_hi", "x_lo",
            "dve_step", "dtT_done", "dt_z", "dt_e", "dt_w", "dt_l", "dA_ready", "cs_done", "cs_a",
            "vT_done", "v_ready", "pads_set", "pads_in", "csT_done", "csT_ready", "cs_stored",
            "gq_ready", "rope_done", "kss_done", "k_rt", "ssq_done", "conv_done", "silu_done", "qst_rt",
            "z_taken", "gq_free")
        x_in = sems(*[f"x_in{i}" for i in range(NT)])
        pair_free = sems("pair_free0", "pair_free1")
        stored = sems("stored0", "stored1")
        PART1_STORES = 16 * 22

        def pair(p):
            return F[:, 2 * p:2 * p + 2, :].rearrange("p b c -> p (b c)")

        X_AHEAD = 5

        def x_banks(i):
            return (M[:, 0:2, :], M[:, 2:4, :], F[:, 2:4, :])[i % 3]

        @block.sync
        def _(sp):
            for i in range(NT):
                sp.dma_start(xrow[:, i, :], a["x"][i * P:(i + 1) * P, :]).then_inc(x_in[i], 16)
                if i == 3:
                    load_w(sp, 0, 0, 0)
            load_w(sp, 1, 0, 0)
            sp.dma_start(cos[:, :], a["cos"]).then_inc(rope_in, 16)
            sp.dma_start(sin[:, :], a["sin"]).then_inc(rope_in, 16)
            for u in range(2, Q0 + 4):
                load_w(sp, u, 0, 0)
            for u in (K0, K0 + 1):
                sp.wait_ge(rope_done, u - K0 + 1)
                sp.dma_start(k_d[u - K0, :, CH:], res[:, u % 2, :]).then_inc(stored[u % 2], 16)
            with nc.sync.Fori(0, 4) as i:
                for s in range(2):
                    load_w(sp, Q0 + 4 + s, 2, i)
                    sp.wait_ge(rope_done, i * 2 + (3 + s))
                    sp.dma_start(q_d[ds(i * 2 + s, 1), :, :], res[:, (Q0 + s) % 2, :]).then_inc(stored[(Q0 + s) % 2], 16)
            with nc.sync.Fori(0, (B2 + 2 - Q0 - 12) // 2) as i:
                for n in range(2):
                    load_w(sp, Q0 + 12 + n, 2, i)

        @block.gpsimd
        def _(pool):
            nc.gpsimd.memset(zpad[:], 0.0).then_inc(pads_set, 1)
            pool.wait_ge(pads_set, 1)
            for kt in range(2):
                pool.dma_start(k_d[kt, :, 0:CH], zpad[:, 0:CH]).then_inc(pads_in, 16)
            pool.dma_start(v_d[0:CH, :], zpad[0:CH, :]).then_inc(pads_in, 16)

            low(pool, 0, 0, 0)
            with nc.gpsimd.Fori(0, (B2 + 1) // 2) as i:
                for n in range(2):
                    low(pool, 1 + n, 2, i)

        @block.scalar
        def _(act):
            act.dma_start(gain[:, :], a["gain"]).then_inc(gain_in, 16)
            act.dma_start(cst[:, :], a["consts"][:, 0:PART1_CONSTS]).then_inc(consts_in, 16)
            act.dma_start(cst1[:, :], a["consts"][:, PART1_CONSTS:]).then_inc(consts_in, 16)
            act.wait_ge(dve_step, 1)
            nc.scalar.activation(neg_a[:, 0:1], eps[:], ACT.Sqrt)
            act.sem_inc(silu_done, 2)

            def x_high(i):
                act.wait_ge(xt_done, i + 1)
                nc.scalar.activation(X0[:, 0, :, i * P:(i + 1) * P], x_banks(i).rearrange("p b (k t) -> p (b k) t", t=P),
                                     ACT.Copy).then_inc(x_hi, 1)

            for i in range(NT):
                act.wait_ge(x_in[i], 16)
                nc.scalar.activation(cv[:, 0, :], xrow[:, i, :], ACT.Square, accum_out=ssx[:, 0, i:i + 1]).then_inc(x_sq, 1)
                act.wait_ge(x_sq, i + 1)
                nc.scalar.activation(ssx[:, 0, i:i + 1], ssx[:, 0, i:i + 1], ACT.Sqrt, bias=eps[:], scale=1.0 / DM).then_inc(x_rt, 1)
                if i == 3:
                    high(act, 0, 0, 0)
                if 1 <= i <= X_AHEAD:
                    x_high(i - 1)
            for i in range(X_AHEAD, NT):
                x_high(i)
            high(act, 1, 0, 0)

            act.wait_ge(consts_in, 32)
            nc.scalar.activation(neg_a[:], C("a_log"), ACT.Exp)
            act.wait_ge(unit_done, 2)
            nc.scalar.activation(staged[0:NHS, 0, :], pair(0)[0:NHS, :], ACT.Copy).then_inc(pair_free[0], 1)
            high(act, 2, 0, 0)

            def stage_v(u):
                act.wait_ge(unit_done, 2 * u + 2)
                nc.scalar.activation(staged[:, u, :], pair(u % 2), ACT.Copy).then_inc(pair_free[u % 2], 1)
                high(act, u + 2, 0, 0)

            def v_out(u, b):
                act.wait_ge(vT_done, u)
                nc.scalar.activation(res[:, u % 2, :], flat(M[:, b:b + 2, :]), ACT.Copy).then_inc(v_ready, 1)
                act.wait_ge(v_ready, u)
                act.dma_start(v_d[CH:, (u - V0) * P:(u - V0 + 1) * P].rearrange("(t p) c -> p t c", p=P),
                              res[:, u % 2, :].rearrange("p (t c) -> p t c", t=NT)).then_inc(stored[u % 2], 16)

            stage_v(V0)
            act.wait_ge(dt_z, 1)
            nc.scalar.activation(small[:, 1], small[:, 1], ACT.Exp).then_inc(dt_e, 1)
            act.wait_ge(dt_w, 1)
            nc.scalar.activation(small[:, 4], small[:, 2], ACT.Ln).then_inc(dt_l, 1)
            stage_v(V0 + 1)
            v_out(V0, 2)
            act.wait_ge(cs_a, 1)
            nc.scalar.activation(de_sb, small[:, 5], ACT.Exp)
            nc.scalar.activation(cd_sb, small[:, 0], ACT.Exp)
            v_out(V0 + 1, 0)
            act.wait_ge(csT_done, 1)
            nc.scalar.activation(csT[:, :], M[0:NHS, 2:4, :].rearrange("p b c -> p (b c)"), ACT.Copy).then_inc(csT_ready, 1)
            act.wait_ge(csT_ready, 1)
            act.dma_start(cs_d[:, :], csT[:, :]).then_inc(cs_stored, 16)
            nc.scalar.activation(ecsT[:, :], csT[:, :], ACT.Exp).then_inc(csT_ready, 1)
            act.wait_ge(csT_ready, 2)
            act.dma_start(ecs_d[:, :], ecsT[:, :]).then_inc(cs_stored, 16)

            def gain_and_square(p, g, done):
                for h in range(2):
                    act.wait_ge(unit_done, done + h)
                    to = slice(h * HALF, (h + 1) * HALF)
                    nc.scalar.activation(gq[:, p, to], F[:, 2 * p + h, :], ACT.Identity, scale=C(g)).then_inc(gq_ready, 1)
                    last = nc.scalar.activation(sq[:, p, to], F[:, 2 * p + h, :], ACT.Square)
                last.then_inc(pair_free[p], 1)

            for u in (K0, K0 + 1):
                gain_and_square(u % 2, "k_gain", 2 * u + 1)
                high(act, u + 2, 0, 0)
            for u in (K0, K0 + 1):
                act.wait_ge(kss_done, u - K0 + 1)
                b = 2 * (u - K0)
                nc.scalar.activation(krms[:, u - K0, :], M[:, b:b + 2, :].rearrange("p b c -> p (b c)"), ACT.Sqrt,
                                     bias=eps[:], scale=1.0 / HD).then_inc(k_rt, 1)
            with nc.scalar.Fori(0, 4) as i:
                for s in range(2):
                    p = (Q0 + s) % 2
                    act.wait_ge(ssq_done, i * 2 + (1 + s))
                    act.wait_ge(gq_free, i * 2 + (1 + s))
                    gain_and_square(p, "q_gain", i * 4 + (2 * (Q0 + s) + 1))
                    high(act, Q0 + s + 2, 2, i)
            act.wait_ge(ssq_done, 10)
            nc.scalar.activation(rq_sb[:].rearrange("p t (b u i) -> p (t b) u i", b=2, u=2),
                                 M[:, 0, 0:NT * NH].rearrange("p (tb i u) -> p tb u i", i=4, u=2), ACT.Sqrt,
                                 bias=eps[:], scale=1.0 / HD).then_inc(qst_rt, 1)
            with nc.scalar.Fori(0, NX // 2) as i:
                for s in range(2):
                    p = (X0U + s) % 2
                    high(act, X0U + s + 2, 2, i)
                    act.wait_ge(conv_done, i * 2 + (s + 1))
                    act.wait_ge(stored[p], i * 16 + 16 * ((X0U + s - 1) // 2))
                    nc.scalar.activation(res[:, p, :], cv[:, p, :], ACT.Silu, bias=C("conv_b")[:, ds(i * 2 + s, 1)]).then_inc(silu_done, 1)
                    act.wait_ge(silu_done, i * 2 + (s + 3))
                    act.dma_start(x_d[ds(i * 2 + s, 1), :, :], res[:, p, :]).then_inc(stored[p], 16)

            with nc.scalar.Fori(0, 4) as i:
                for s in range(2):
                    p = (Z0 + s) % 2
                    act.wait_ge(unit_done, i * 4 + (2 * (Z0 + s) + 2))
                    act.wait_ge(stored[p], i * 16 + 16 * ((Z0 + s - 1) // 2))
                    nc.scalar.activation(res[:, p, :], pair(p), ACT.Silu).then_inc(z_taken, 1)
                    high(act, Z0 + s + 2, 2, i)
                    act.wait_ge(z_taken, i * 2 + (s + 1))
                    act.sem_inc(pair_free[p], 1)
                    act.dma_start(z_d[ds(i * 2 + s, 1), :, :], res[:, p, :]).then_inc(stored[p], 16)

        @block.vector
        def _(dve):
            ch = Chain(dve, dve_step)
            ch.link(nc.vector.memset(eps[:], EPS))

            def x_low(i):
                dve.wait_ge(x_hi, i + 1)
                to = slice(i * P, (i + 1) * P)
                nc.vector.tensor_tensor(X0[:, 1, :, to], x_banks(i).rearrange("p b (k t) -> p (b k) t", t=P),
                                        X0[:, 0, :, to].bitcast(f32), ALU.subtract).then_inc(x_lo, 1)

            dve.wait_ge(gain_in, 16)
            for i in range(NT):
                dve.wait_ge(x_rt, i + 1)
                ch.link(nc.vector.reciprocal(ssx[:, 1, i:i + 1], ssx[:, 0, i:i + 1]))
                nc.vector.scalar_tensor_tensor(xrow[:, i, :], xrow[:, i, :], ssx[:, 1, i:i + 1], gain[:],
                                               ALU.mult, ALU.mult).then_inc(xn_ready, 1)
                if 1 <= i <= X_AHEAD:
                    x_low(i - 1)
            for i in range(X_AHEAD, NT):
                x_low(i)

            z, e, w, d, ln, t5 = (small[:, n] for n in range(6))

            def per_tile(name):
                return C(name).unsqueeze(1).to_broadcast([P, NT, NHS])

            dve.wait_ge(dtT_done, 1)
            dve.wait_ge(consts_in, 32)
            ch.link(nc.vector.tensor_tensor(z, M[:, 0, 0:NT * NHS].rearrange("p (t h) -> p t h", t=NT), per_tile("dt_bias"), ALU.add))
            nc.vector.scalar_tensor_tensor(e, z, -1.0, z, ALU.mult, ALU.min).then_inc(dt_z, 1)
            dve.wait_ge(dt_e, 1)
            ch.link(nc.vector.tensor_scalar(w, e, 1.0, None, ALU.add))
            dve.sem_inc(dt_w, 1)
            ch.link(nc.vector.tensor_scalar(d, w, 1.0, None, ALU.subtract))
            ch.link(nc.vector.tensor_scalar(t5, d, 0.0, None, ALU.is_equal))
            ch.link(nc.vector.tensor_tensor(d, d, t5, ALU.add))
            ch.link(nc.vector.reciprocal(d, d))
            ch.link(nc.vector.tensor_tensor(d, d, e, ALU.mult))
            dve.wait_ge(dt_l, 1)
            ch.link(nc.vector.tensor_tensor(ln, ln, d, ALU.mult))
            ch.link(nc.vector.tensor_tensor(t5, t5, e, ALU.mult))
            ch.link(nc.vector.tensor_tensor(ln, ln, t5, ALU.add))
            ch.link(nc.vector.scalar_tensor_tensor(dt_sb, z, 0.0, ln, ALU.max, ALU.add))
            ch.link(nc.vector.tensor_scalar(neg_a[:], neg_a[:], -1.0, None, ALU.mult))
            nc.vector.tensor_tensor(z, dt_sb, neg_a[:].unsqueeze(1).to_broadcast([P, NT, NHS]), ALU.mult).then_inc(dA_ready, 1)
            dve.wait_ge(cs_done, 1)
            ch.link(nc.vector.tensor_copy(cs_sb, M[:, 0, 0:NT * NHS].rearrange("p (t h) -> p t h", t=NT)))
            ch.link(nc.vector.tensor_copy(z, M[:, 1, 0:NT * NHS].rearrange("p (t h) -> p t h", t=NT)))
            nc.vector.tensor_tensor(t5, z, cs_sb, ALU.subtract).then_inc(cs_a, 1)

            def rotate(p, gq_count, slot_stored, norm=None, steps=4):
                dve.wait_ge(gq_ready, gq_count)
                for b in (0, 64):
                    for src, dst in ((b, b + 32), (b + 32, b)):
                        sw = nc.vector.tensor_tensor(cv[dst:dst + 32, p, :], gq[src:src + 32, p, :], sin[src:src + 32, :], ALU.mult)
                ch.link(sw)
                dve.wait_ge(stored[p], slot_stored)
                ch.link(nc.vector.tensor_tensor(res[:, p, :], gq[:, p, :], cos[:], ALU.mult))
                dve.sem_inc(gq_free, 1)
                last = nc.vector.tensor_tensor(res[:, p, :], res[:, p, :], cv[:, p, :], ALU.add)
                if norm is None:
                    last.then_inc(rope_done, 1)
                else:
                    ch.link(last)

            dve.wait_ge(rope_in, 32)
            for u in (K0, K0 + 1):
                rotate(u % 2, 2 * (u - K0 + 1), 16 * ((u - 1) // 2), norm=True)
            for u in (K0, K0 + 1):
                dve.wait_ge(k_rt, u - K0 + 1)
                ch.link(nc.vector.reciprocal(krms[:, u - K0, :], krms[:, u - K0, :]))
                nc.vector.tensor_tensor(res[:, u % 2, :], res[:, u % 2, :], krms[:, u - K0, :], ALU.mult).then_inc(rope_done, 1)
            for i in ch.loop(nc.vector.Fori, 4, 4):
                for s in range(2):
                    rotate((Q0 + s) % 2, i * 4 + (2 * s + 6), i * 16 + 16 * ((Q0 + s - 1) // 2))
            dve.wait_ge(qst_rt, 1)
            ch.link(nc.vector.reciprocal(rq_sb[:], rq_sb[:]))
            nc.vector.tensor_scalar(rq_sb[:], rq_sb[:], HD ** -0.5, None, ALU.mult)
            cw = C("conv_w").rearrange("p (n k) -> p n k", k=4)
            for i in ch.loop(nc.vector.Fori, NX // 2, 6):
                for s in range(2):
                    p = (X0U + s) % 2
                    acc, raw = cv[:, p, :], pair(p)

                    def tap(k):
                        return cw[:, ds(i * 2 + s, 1), k:k + 1].rearrange("p a b -> p (a b)")

                    dve.wait_ge(unit_done, i * 4 + (2 * (X0U + s) + 2))
                    dve.wait_ge(silu_done, i * 2 + s + 1)
                    ch.link(nc.vector.tensor_scalar(acc, raw, tap(3), None, ALU.mult))
                    for back in (1, 2, 3):
                        ins = nc.vector.scalar_tensor_tensor(acc[:, back:], raw[:, 0:T - back], tap(3 - back), acc[:, back:], ALU.mult, ALU.add)
                        if back < 3:
                            ch.link(ins)
                    ins.then_inc(conv_done, 1)
                    dve.wait_ge(conv_done, i * 2 + (s + 1))
                    dve.sem_inc(pair_free[p], 1)

        @block.tensor
        def _(pe):
            pe.sem_inc(ssq_done, 2)
            pe.wait_ge(consts_in, 32)
            for i in range(NT):
                pe.wait_ge(xn_ready, i + 1)
                if i >= 3:
                    pe.wait_ge(x_lo, i - 2)
                for k in range(NK):
                    last = nc.tensor.transpose(x_banks(i)[:, k // 4, (k % 4) * P:(k % 4 + 1) * P],
                                               xrow[:, i, k * P:(k + 1) * P], C("ident"))
                last.then_inc(xt_done, 1)
                if i == NT // 2:
                    pe.wait_ge(x_lo, NT // 2)
                    pe.wait_ge(w_hi, 1)
                    pe.wait_ge(w_lo, 1)
                    matmuls(F[:, 0, :], 0, X0, 0).then_inc(unit_done, 1)

            def unit(p, hi, free):
                pe.wait_ge(w_hi, hi)
                pe.wait_ge(w_lo, hi)
                if free is not None:
                    pe.wait_ge(pair_free[p], free)
                for h in range(2):
                    matmuls(F[:, 2 * p + h, :], p, X0, h).then_inc(unit_done, 1)

            def v_rows(u, b):
                pe.wait_ge(pair_free[u % 2], u // 2 + 1)
                for t in range(NT):
                    last = nc.tensor.transpose(M[:, b + t // 4, (t % 4) * P:(t % 4 + 1) * P],
                                               staged[:, u, t * P:(t + 1) * P], C("ident"))
                last.then_inc(vT_done, 1)

            pe.wait_ge(x_lo, NT)
            matmuls(F[:, 1, :], 0, X0, 1).then_inc(unit_done, 1)
            unit(V0 % 2, V0 + 1, None)
            pe.wait_ge(pair_free[0], 1)
            for t in range(NT):
                last = nc.tensor.transpose(M[:, 0, t * NHS:(t + 1) * NHS], staged[0:NHS, 0, t * P:(t + 1) * P], C("ident")[0:NHS, 0:NHS])
            last.then_inc(dtT_done, 1)
            unit(0, V0 + 2, 1)
            v_rows(V0, 2)
            pe.wait_ge(dA_ready, 1)
            dA = small[:, 0].rearrange("p t h -> p (t h)")
            nc.tensor.matmul(M[:, 0, 0:NT * NHS], C("tri"), dA, start=True, stop=True)
            nc.tensor.matmul(M[:, 1, 0:NT * NHS], C("ones"), dA, start=True, stop=True).then_inc(cs_done, 1)
            unit(1, K0 + 1, 1)
            pe.wait_ge(cs_a, 1)
            v_rows(V0 + 1, 0)
            pe.wait_ge(v_ready, 1)
            for t in range(NT):
                last = nc.tensor.transpose(M[0:NHS, 2 + t // 4, (t % 4) * P:(t % 4 + 1) * P], cs_sb[:, t, :], C("ident"))
            last.then_inc(csT_done, 1)
            unit(0, K0 + 2, 2)
            pe.wait_ge(v_ready, 2)
            pe.wait_ge(csT_ready, 1)
            for u in (K0, K0 + 1):
                pe.wait_ge(pair_free[u % 2], u // 2 + 1)
                for h in range(2):
                    last = nc.tensor.matmul(M[:, 2 * (u - K0) + h, :], C("head_ones"), sq[:, u % 2, h * HALF:(h + 1) * HALF], start=True, stop=True)
                last.then_inc(kss_done, 1)
            with nc.tensor.Fori(0, 4) as i:
                for s in range(2):
                    unit((Q0 + s) % 2, i * 2 + (Q0 + s + 1), i + (Q0 + s) // 2)
                for s in range(2):
                    p = (Q0 + s) % 2
                    pe.wait_ge(pair_free[p], i + ((Q0 + s) // 2 + 1))
                    if s == 0:
                        pe.wait_ge(k_rt, 2)
                    for t in range(NT):
                        last = nc.tensor.matmul(M[:, 0, ds(i * 4 + (t * NH + 2 * s), 2)], sq[:, p, t * P:(t + 1) * P], C("head_sel"), start=True, stop=True)
                    last.then_inc(ssq_done, 1)
            with nc.tensor.Fori(0, NX // 2) as i:
                for s in range(2):
                    unit((X0U + s) % 2, i * 2 + (X0U + s + 1), i + (X0U + s) // 2)
            with nc.tensor.Fori(0, 4) as i:
                for s in range(2):
                    unit((Z0 + s) % 2, i * 2 + (Z0 + s + 1), i + (Z0 + s) // 2)

        qs, w = carve(X1_low, 0, 8, P)
        ks, w = carve(X1_low, w, 2, CH + P)
        vs, w = carve(X1_low, w, 2, NKV * HD)
        xb, w = carve(X1_low, w, 16, P)
        probs, w = carve(X1_low, w, 2, 4, P)
        orow = probs.rearrange("p n c m -> p n (c m)")
        zo, w = carve(X1_low, w, 8, P)
        negm, w = carve(X1_low, w, NH)
        stat, w = carve(X1_low, w, 6, NH)
        assert w <= (NK - 1) * T
        pT, w = carve(X1_low, (NK - 1) * T, 2, 4, P)
        ytmp, _ = carve(X1_low, (NK - 1) * T, 512)
        dec, w = carve(X1_high, 0, 2, HG, P)
        xdt, w = carve(X1_high, w, GROUPS, 512)
        xdd, w = carve(X1_high, w, GROUPS, 512)
        brow, w = carve(X1_high, w, GROUPS, P)
        cbm, w = carve(X1_high, w, GROUPS, P)
        bc, w = carve(X1_high, w, 8, P)
        csb, w = carve(acc_all, 0, NHS, P)
        ecsb, w = carve(acc_all, w, 16, P)
        yo, w = carve(acc_all, w, 16, P)
        state, _ = carve(part[:, :, :].rearrange("p s t -> p (s t)"), 0, GROUPS, 512)
        F2, O, S, Tb = F[:, 2:4], F[:, 0:2], M[:, 0:2], M[:, 2:4]
        (sc_done, xr_done, pt_done, pv_done, brt_done, cb_done, ot_done, yg_done, st_done) = sems(
            "sc_done", "xr_done", "pt_done", "pv_done", "brt_done", "cb_done", "ot_done", "yg_done", "st_done")
        (step2, negm_ready, sinkm_ready, rsum_ready, xdt_ready, orow_ready, cbm_ready, seg_ready, wT_ready, y_taken,
         state_ready, yout_ready) = sems(
            "step2", "negm_ready", "sinkm_ready", "rsum_ready", "xdt_ready", "orow_ready", "cbm_ready", "seg_ready", "wT_ready",
            "y_taken", "state_ready", "yout_ready")
        (probs_ready, sinke_ready, pT_ready, brow_ready, oT_ready, dec_ready, half_taken) = sems(
            "probs_ready", "sinke_ready", "pT_ready", "brow_ready", "oT_ready", "dec_ready", "half_taken")
        (xd_ready, xdd_ready, sdec_ready) = sems("xd_ready", "xdd_ready", "sdec_ready")
        (q_in, k_in, x2_in, v_in, bc_in, cs_in, ecs_in, z_in, o_stored, y_stored) = sems(
            "q_in", "k_in", "x2_in", "v_in", "bc_in", "cs_in", "ecs_in", "z_in", "o_stored", "y_stored")


        @block.sync
        def _(sp):
            for sem, credit in ((sc_done, 1), (xr_done, 1), (pv_done, 1), (yg_done, 1), (ot_done, 2), (xd_ready, 1), (seg_ready, 1),
                                (yout_ready, 1), (y_taken, 1), (oT_ready, 2), (o_stored, 16)):
                sp.sem_inc(sem, credit)
            for p in range(2):
                sp.wait_ge(stored[p], PART1_STORES - 4 * 16)
            sp.wait_ge(pads_in, 48)
            sp.wait_ge(cs_stored, 32)
            with nc.sync.Fori(0, NT) as j:
                at_j = sp.snap(j * P)
                sp.wait_ge(sc_done, j * 4 + 1)
                sp.dma_start(qs[:], q_d[:, :, ds(at_j, P)].rearrange("n p t -> p n t")).then_inc(q_in, 16)
                sp.dma_start(ks[:], k_d[:, :, ds(at_j, CH + P)].rearrange("n p t -> p n t")).then_inc(k_in, 16)
                sp.wait_ge(xr_done, j * 4 + 1)
                sp.wait_ge(xd_ready, j * 4 + 1)
                sp.dma_start(xb[:], x_d[0:16, :, ds(at_j, P)].rearrange("n p t -> p n t")).then_inc(x2_in, 16)
                sp.wait_ge(pv_done, j * 2 + 1)
                for half in range(2):
                    sp.dma_start(vs[:, half, :], v_d[ds(at_j + half * CH, P), :]).then_inc(v_in, 16)
                load_w(sp, B2 + 2, 4, j)
                sp.wait_ge(yg_done, j * 4 + 1)
                sp.dma_start(bc[:], x_d[16:24, :, ds(at_j, P)].rearrange("n p t -> p n t")).then_inc(bc_in, 16)
                sp.wait_ge(seg_ready, j * 4 + 1)
                sp.dma_start(csb[:], cs_d[:, ds(at_j, P)].partition_broadcast(P)).then_inc(cs_in, 16)
                sp.wait_ge(yout_ready, j * 4 + 1)
                for h in range(2):
                    sp.dma_start(ecsb[HD * h:HD * h + HD],
                                 ecs_d.rearrange("(n u) t -> u n t", u=2)[h, :, ds(at_j, P)].partition_broadcast(HD)).then_inc(ecs_in, 16)
                sp.wait_ge(o_stored, j * 16 + 16)
                for p in range(2):
                    sp.wait_ge(stored[p], PART1_STORES)
                sp.dma_start(zo[:], z_d[0:8, :, ds(at_j, P)].rearrange("n p t -> p n t")).then_inc(z_in, 16)
                for n in range(3, 6):
                    load_w(sp, B2 + n, 4, j)

        @block.tensor
        def _(pe):
            pe.wait_ge(pair_free[1], 22)
            with nc.tensor.Fori(0, NT) as j:
                def at(n, k):
                    return j * n + k

                def scores(r):
                    u = r % 2
                    for c in range(4):
                        for half in range(2):
                            last = nc.tensor.matmul(S[64 * half:64 * half + 64, u, c * P:(c + 1) * P],
                                                    qs[64 * u:64 * u + 64, 4 * (r // 2) + c, 64 * half:64 * half + 64],
                                                    ks[64 * u:64 * u + 64, r // 2, 64 * half:64 * half + P], start=True, stop=True)
                    last.then_inc(sc_done, 1)

                def transpose4(bank, src, done):
                    for c in range(4):
                        last = nc.tensor.transpose(bank[:, c * P:(c + 1) * P], src(c), C("ident"))
                    last.then_inc(done, 1)

                def x_rows(r):
                    if r == 0:
                        pe.wait_ge(q_in, at(16, 16))
                        pe.wait_ge(k_in, at(16, 16))
                        pe.wait_ge(state_ready, at(4, 1))
                        pe.wait_ge(x2_in, at(16, 16))
                    if r < 2:
                        pe.wait_ge(oT_ready, at(2, 1 + r))
                    else:
                        pe.wait_ge(pT_ready, at(4, r + 1))
                    transpose4(Tb[:, r % 2, :], lambda c: xb[:, 4 * r + c, :], xr_done)

                def probs_T(r):
                    pe.wait_ge(probs_ready, at(4, r + 1))
                    if r < 2:
                        pe.wait_ge(xdt_ready, at(4, r + 1))
                    else:
                        pe.wait_ge(pT_ready, at(4, r - 1))
                    transpose4(Tb[:, r % 2, :], lambda c: probs[:, r % 2, c, :], pt_done)

                def attend(r):
                    pe.wait_ge(pT_ready, at(4, r + 1))
                    if r == 0:
                        pe.wait_ge(v_in, at(32, 32))
                        pe.wait_ge(y_taken, at(4, 1))
                    b = r // 2
                    for c in range(4):
                        to = (4 * (r % 2) + c) * HD
                        for half in range(2):
                            last = nc.tensor.matmul(O[64 * half:64 * half + 64, b, to:to + HD],
                                                    pT[:, r % 2, c, 64 * half:64 * half + 64],
                                                    vs[:, half, r * HD:(r + 1) * HD], start=True, stop=True)
                    if r % 2:
                        last.then_inc(pv_done, 1)

                def o_T(b):
                    pe.wait_ge(orow_ready, at(2, b + 1))
                    pe.wait_ge(xdt_ready, at(4, 3 + b))
                    transpose4(Tb[:, b, :], lambda c: orow[:, b, c * P:(c + 1) * P], ot_done)

                def b_rows_and_cb():
                    pe.wait_ge(bc_in, at(16, 16))
                    pe.wait_ge(probs_ready, at(4, 4))
                    transpose4(S[:, 0, :], lambda c: bc[:, c, :], brt_done)
                    for g in range(GROUPS):
                        last = nc.tensor.matmul(S[:, 1, g * P:(g + 1) * P], bc[:, g, :], bc[:, 4 + g, :], start=True, stop=True)
                    last.then_inc(cb_done, 1)

                def group(g):
                    pe.wait_ge(wT_ready, at(4, g + 1))
                    if g == 0:
                        pe.wait_ge(orow_ready, at(2, 2))
                    else:
                        pe.wait_ge(y_taken, at(4, g + 1))
                    for h in range(HG):
                        nc.tensor.matmul(O[HD * (h % 2):HD * (h % 2) + HD, 0, (h // 2) * P:(h // 2 + 1) * P],
                                         xdt[:, g, h * HD:(h + 1) * HD], dec[:, g % 2, h, :], start=True, stop=True)
                    for c in range(4):
                        last = nc.tensor.matmul(O[:, 1, c * P:(c + 1) * P], state[:, g, c * P:(c + 1) * P], bc[:, 4 + g, :],
                                                start=True, stop=True)
                    last.then_inc(yg_done, 1)
                    pe.wait_ge(xdd_ready, at(4, g + 1))
                    if g == 0:
                        pe.wait_ge(brow_ready, at(1, 1))
                    elif g == 1:
                        pe.wait_ge(cbm_ready, at(1, 1))
                    else:
                        pe.wait_ge(state_ready, at(4, g))
                    nc.tensor.matmul(S[:, g % 2, :], brow[:, g, :], xdd[:, g, :], start=True, stop=True).then_inc(st_done, 1)

                def half_unit(h):
                    n = h // 2
                    if h % 2 == 0:
                        pe.wait_ge(w_hi, at(4, B2 + n + 1))
                        pe.wait_ge(w_lo, at(4, B2 + n + 1))
                    pe.wait_ge(half_taken, at(8, h + 1))
                    matmuls(F2[:, h % 2, :], (B2 + n) % 2, X0, h % 2).then_inc(unit_done, 1)

                x_rows(0)
                x_rows(1)
                scores(0)
                scores(1)
                half_unit(0)
                probs_T(0)
                probs_T(1)
                scores(2)
                scores(3)
                half_unit(1)
                attend(0)
                attend(1)
                probs_T(2)
                probs_T(3)
                half_unit(2)
                attend(2)
                attend(3)
                x_rows(2)
                x_rows(3)
                b_rows_and_cb()
                half_unit(3)
                o_T(0)
                o_T(1)
                group(0)
                half_unit(4)
                group(1)
                half_unit(5)
                group(2)
                half_unit(6)
                group(3)
                half_unit(7)

        @block.vector
        def _(dve):
            ch = Chain(dve, step2)
            nc.vector.memset(state[:], 0.0).then_inc(state_ready, 1)
            ch.link(nc.vector.tensor_scalar(stat[:, 5, :], C("sinks"), -1.0, None, ALU.mult))
            for j in ch.loop(nc.vector.Fori, NT, 4 * 3 + 1 + 4):
                def at(n, k):
                    return j * n + k

                def per_head(ap, lo, n, width=HD):
                    return ap[:, ds(j, 1), lo:lo + n].rearrange("p a h -> p (a h)").unsqueeze(2).to_broadcast([P, n, width])

                def maxima(r):
                    dve.wait_ge(sc_done, at(4, r + 2))
                    bank = S[:, r % 2, :].rearrange("p (c m) -> p c m", c=4)
                    ch.link(nc.vector.tensor_scalar(bank[0:CH, :, 0:CH], bank[0:CH, :, 0:CH],
                                                    C("pad_mask")[0:CH, ds(j, 1)], None, ALU.add))
                    h4 = slice(4 * r, 4 * r + 4)
                    ch.link(nc.vector.tensor_reduce(stat[:, 0, h4], bank, AX.X, ALU.max))
                    ch.link(nc.vector.scalar_tensor_tensor(stat[:, 1, h4], stat[:, 0, h4], -1.0,
                                                           rq_sb[:, ds(j, 1), h4].rearrange("p a h -> p (a h)"), ALU.mult, ALU.mult))
                    nc.vector.tensor_tensor(negm[:, h4], stat[:, 1, h4], stat[:, 5, h4], ALU.min).then_inc(negm_ready, 1)

                def x_dt(r):
                    dve.wait_ge(xr_done, at(4, r + 2))
                    nc.vector.tensor_tensor(xdt[:, r, :].rearrange("p (h d) -> p h d", d=HD),
                                            Tb[:, r % 2, :].rearrange("p (h d) -> p h d", d=HD),
                                            per_head(dt_sb, 8 * r, 8), ALU.mult).then_inc(xdt_ready, 1)

                def seg(g):
                    if g == 0:
                        dve.wait_ge(cs_in, at(16, 16))
                    if g >= 2:
                        dve.wait_ge(yg_done, at(4, g))
                    for h in range(HG):
                        last = nc.vector.tensor_scalar(dec[:, g % 2, h, :], csb[:, HG * g + h, :],
                                                       cs_sb[:, ds(j, 1), HG * g + h:HG * g + h + 1].rearrange("p a h -> p (a h)"),
                                                       0.0, ALU.subtract, ALU.min)
                    last.then_inc(seg_ready, 1)

                def o_rows(b):
                    dve.wait_ge(pv_done, at(2, b + 2))
                    dve.wait_ge(pt_done, at(4, 4))
                    inv = stat[:, 4, 8 * b:8 * b + 8].unsqueeze(2).to_broadcast([P, 8, HD])
                    nc.vector.tensor_tensor(orow[:, b, :].rearrange("p (h d) -> p h d", d=HD),
                                            O[:, b, :].rearrange("p (h d) -> p h d", d=HD), inv, ALU.mult).then_inc(orow_ready, 1)

                def o_out(b):
                    if b == 0:
                        dve.wait_ge(z_in, at(16, 16))
                    dve.wait_ge(ot_done, at(2, b + 3))
                    to = flat(zo[:, 4 * b:4 * b + 4, :])
                    nc.vector.tensor_tensor(to, to, Tb[:, b, :], ALU.mult).then_inc(oT_ready, 1)

                def weights_T(g):
                    dve.wait_ge(dec_ready, at(4, g + 1))
                    nc.vector.tensor_tensor(dec[:, g % 2], dec[:, g % 2], cbm[:, g, :].unsqueeze(1).to_broadcast([P, HG, P]),
                                            ALU.mult).then_inc(wT_ready, 1)

                def y_out(g):
                    to = flat(yo[:, 4 * g:4 * g + 4, :])
                    dve.wait_ge(yg_done, at(4, g + 2))
                    if g == 0:
                        dve.wait_ge(xd_ready, at(4, 5))
                        dve.wait_ge(ecs_in, at(32, 32))
                    ch.link(nc.vector.tensor_tensor(to, to, O[:, 0, :], ALU.add))
                    nc.vector.tensor_tensor(ytmp[:], O[:, 1, :], flat(ecsb[:, 4 * g:4 * g + 4, :]), ALU.mult).then_inc(y_taken, 1)
                    dve.wait_ge(y_taken, at(4, g + 2))
                    nc.vector.tensor_tensor(to, to, ytmp[:], ALU.add).then_inc(yout_ready, 1)

                def add_state(g):
                    dve.wait_ge(st_done, at(4, g + 1))
                    dve.wait_ge(sdec_ready, at(4, g + 1))
                    nc.vector.tensor_tensor(state[:, g, :], state[:, g, :], S[:, g % 2, :], ALU.add).then_inc(state_ready, 1)

                maxima(0)
                maxima(1)
                x_dt(0)
                x_dt(1)
                maxima(2)
                maxima(3)
                dve.wait_ge(negm_ready, at(4, 4))
                nc.vector.tensor_tensor(stat[:, 3, :], C("sinks"), negm[:], ALU.add).then_inc(sinkm_ready, 1)
                seg(0)
                seg(1)
                dve.wait_ge(sinke_ready, at(1, 1))
                ch.link(nc.vector.tensor_tensor(stat[:, 3, :], stat[:, 3, :], stat[:, 2, :], ALU.add))
                nc.vector.reciprocal(stat[:, 4, :], stat[:, 3, :]).then_inc(rsum_ready, 1)
                dve.wait_ge(rsum_ready, at(1, 1))
                o_rows(0)
                o_rows(1)
                x_dt(2)
                x_dt(3)
                dve.wait_ge(cb_done, at(1, 1))
                nc.vector.tensor_tensor(cbm[:], S[:, 1, :].rearrange("p (g l) -> p g l", g=GROUPS),
                                        C("tri").unsqueeze(1).to_broadcast([P, GROUPS, P]), ALU.mult).then_inc(cbm_ready, 1)
                dve.wait_ge(cbm_ready, at(1, 1))
                weights_T(0)
                weights_T(1)
                o_out(0)
                o_out(1)
                for g in range(GROUPS):
                    y_out(g)
                    if g + 2 < GROUPS:
                        seg(g + 2)
                    add_state(g)
                    if g + 2 < GROUPS:
                        weights_T(g + 2)

        @block.scalar
        def _(act):
            act.sem_inc(half_taken, 2)
            with nc.scalar.Fori(0, NT) as j:
                def at(n, k):
                    return j * n + k

                def exps(r):
                    act.wait_ge(negm_ready, at(4, r + 1))
                    if r < 2:
                        act.wait_ge(ot_done, at(2, r + 1))
                    for c in range(4):
                        h = 4 * r + c
                        last = nc.scalar.activation(probs[:, r % 2, c, :], S[:, r % 2, c * P:(c + 1) * P], ACT.Exp,
                                                    bias=negm[:, h:h + 1], scale=rq_sb[:, ds(j, 1), h:h + 1].rearrange("p a h -> p (a h)"),
                                                    accum_out=stat[:, 2, h:h + 1])
                    last.then_inc(probs_ready, 1)

                def probs_out(r):
                    act.wait_ge(pt_done, at(4, r + 1))
                    if r >= 2:
                        act.wait_ge(pv_done, at(2, 2))
                    if r == 0:
                        act.wait_ge(yout_ready, at(4, 1))
                    nc.scalar.activation(flat(pT[:, r % 2]), Tb[:, r % 2, :], ACT.Copy).then_inc(pT_ready, 1)

                def decay(g):
                    act.wait_ge(seg_ready, at(4, g + 2))
                    nc.scalar.activation(dec[:, g % 2], dec[:, g % 2], ACT.Exp).then_inc(dec_ready, 1)

                def take_half(h):
                    n, p = h // 2, (h // 2) % 2
                    act.wait_ge(unit_done, at(8, 2 * B2 + h + 1))
                    if h % 2 == 0:
                        act.wait_ge(stored[p], at(32, 16 * (n // 2) + PART1_STORES))
                    nc.scalar.activation(res[:, p, (h % 2) * HALF:(h % 2 + 1) * HALF], F2[:, h % 2, :], ACT.Copy).then_inc(half_taken, 1)
                    if h % 2:
                        high(act, B2 + n + 2, 4, j)
                        act.wait_ge(half_taken, at(8, h + 3))
                        to = z_d[ds(j * 2 + (8 + n), 1)] if n < 2 else g_d[ds(j * 2 + (n - 2), 1)]
                        act.dma_start(to, res[:, p, :]).then_inc(stored[p], 16)

                exps(0)
                exps(1)
                take_half(0)
                probs_out(0)
                probs_out(1)
                exps(2)
                exps(3)
                act.wait_ge(sinkm_ready, at(1, 1))
                nc.scalar.activation(stat[:, 3, :], stat[:, 3, :], ACT.Exp).then_inc(sinke_ready, 1)
                take_half(1)
                probs_out(2)
                probs_out(3)
                decay(0)
                decay(1)
                take_half(2)
                act.wait_ge(brt_done, at(1, 1))
                nc.scalar.activation(flat(brow[:]), S[:, 0, :], ACT.Copy).then_inc(brow_ready, 1)
                take_half(3)
                take_half(4)
                act.wait_ge(oT_ready, at(2, 4))
                act.dma_start(o_d[:, :, ds(j * P, P)].rearrange("n p t -> p n t"), zo[:]).then_inc(o_stored, 16)
                decay(2)
                take_half(5)
                decay(3)
                take_half(6)
                take_half(7)

        @block.gpsimd
        def _(pool):
            with nc.gpsimd.Fori(0, NT) as j:
                def at(n, k):
                    return j * n + k

                def per_head(ap, lo, n):
                    return ap[:, ds(j, 1), lo:lo + n].rearrange("p a h -> p (a h)").unsqueeze(2).to_broadcast([P, n, HD])

                def x_dd(g):
                    pool.wait_ge(xdt_ready, at(4, g + 1))
                    nc.gpsimd.tensor_tensor(xdd[:, g, :].rearrange("p (h d) -> p h d", d=HD),
                                            xdt[:, g, :].rearrange("p (h d) -> p h d", d=HD),
                                            per_head(de_sb, HG * g, HG), ALU.mult).then_inc(xdd_ready, 1)

                def decay_state(g):
                    pool.wait_ge(yg_done, at(4, g + 2))
                    to = state[:, g, :].rearrange("p (h d) -> p h d", d=HD)
                    nc.gpsimd.tensor_tensor(to, to, per_head(cd_sb, HG * g, HG), ALU.mult).then_inc(sdec_ready, 1)

                pool.wait_ge(x2_in, at(16, 16))
                nc.gpsimd.tensor_tensor(yo[:], xb[:], C("d_skip").unsqueeze(2).to_broadcast([P, 16, P]), ALU.mult).then_inc(xd_ready, 4)
                x_dd(0)
                x_dd(1)
                low(pool, B2 + 0 + 2, 4, j)
                x_dd(2)
                x_dd(3)
                low(pool, B2 + 1 + 2, 4, j)
                decay_state(0)
                decay_state(1)
                low(pool, B2 + 2 + 2, 4, j)
                decay_state(2)
                decay_state(3)
                low(pool, B2 + 3 + 2, 4, j)
                pool.wait_ge(yout_ready, at(4, 5))
                pool.dma_start(y_d[:, :, ds(j * P, P)].rearrange("n p t -> p n t"), yo[:]).then_inc(y_stored, 16)
                pool.wait_ge(y_stored, at(16, 16))

        gate = res
        ms = ssd_sb[:, :].rearrange("p n t h -> p (n t h)")
        (step3, silu3, gated, y_sq, sq_done, act_hi, act_lo, gateA_ready, gateB_ready, gr_ready, ms_done, ms_rt, rms_ready,
         acc_ready, m_hi, m_lo, rows_in, row_done, out_ready, out_stored) = sems(
            "step3", "silu3", "gated", "y_sq", "sq_done", "act_hi", "act_lo", "gateA_ready", "gateB_ready", "gr_ready",
            "ms_done", "ms_rt", "rms_ready", "acc_ready", "m_hi", "m_lo", "rows_in", "row_done", "out_ready", "out_stored")
        o_in = sems(*[f"o_in{k}" for k in range(NK)])
        gateA_in = sems("gateA_in0", "gateA_in1")
        y_in = sems("y_in0", "y_in1")
        merge_in = sems("merge_in0", "merge_in1")
        a_stored = sems("a_stored0", "a_stored1")
        pair3_free = sems("pair3_free0", "pair3_free1")

        DVE_TILES = 2

        def pair3(p):
            return F[:, 2 * p:2 * p + 2, :].rearrange("p b c -> p (b c)")

        def row_bank(t):
            return M[:, t, :] if t < 4 else F[:, t - 4, :]

        def tile(X, part, i, s=0):
            return X[:, part, ds(i * 2 + s, 1), :].rearrange("p a t -> p (a t)").bitcast(f32)

        def split_tile(X, part, i, s):
            return X[:, part, ds(i * 2 + s, 1), :].rearrange("p a t -> p (a t)")

        def column(name, i, s):
            return C(name)[:, ds(i * 2 + s, 1)]

        def acc_tile(i, s):
            return acc[:, ds(i * 2 + s, 1), :].rearrange("p a t -> p (a t)")

        def row(ap):
            return ap.rearrange("a p t -> (a p) t")


        @block.sync
        def _(sp):
            def load_gateA(i, s):
                sp.dma_start(acc_tile(i, s), row(g_d[ds(i * 2 + s, 1)])).then_inc(gateA_in[s], 16)

            def load_y(X, q0, i, s):
                sp.dma_start(tile(X, 1, i, s), row(y_d[ds(i * 2 + (q0 + s), 1)])).then_inc(y_in[s], 16)
                sp.dma_start(tile(X, 0, i, s), row(z_d[ds(i * 2 + (8 + q0 + s), 1)])).then_inc(y_in[s], 16)

            def load_merge(i, s):
                sp.dma_start(gate[:, s, :], row(g_d[ds(i * 2 + (8 + s), 1)])).then_inc(merge_in[s], 16)
                sp.dma_start(part[:, s, :], row(a_d[ds(i * 2 + s, 1)])).then_inc(merge_in[s], 16)

            for s in range(2):
                sp.sem_inc(a_stored[s], 16)
            sp.wait_ge(o_stored, 16 * (NT + 1))
            sp.wait_ge(xd_ready, 4 * NT + 1)
            for k in range(NK - 1):
                sp.dma_start(X1[:, 1, k, :].bitcast(f32), o_d[k]).then_inc(o_in[k], 16)
            sp.wait_ge(yout_ready, 4 * NT + 1)
            sp.dma_start(X1[:, 1, NK - 1, :].bitcast(f32), o_d[NK - 1]).then_inc(o_in[NK - 1], 16)
            for s in range(2):
                load_w(sp, B3 + 2 + s, 0, 0)
            for p in range(2):
                sp.wait_ge(stored[p], PART1_STORES + 32 * NT)
            sp.wait_ge(y_stored, 16 * NT)
            for s in range(2):
                load_gateA(0, s)
                load_y(X0, 0, 0, s)
            with nc.sync.Fori(0, 3) as i:
                for s in range(2):
                    sp.wait_ge(gateA_ready, i * 2 + (s + 1))
                    load_gateA(i + 1, s)
                    sp.wait_ge(act_lo, i * 2 + (NK + s + 1))
                    load_y(X0, 0, i + 1, s)
                    load_w(sp, B3 + 4 + s, 2, i)
            for s in range(2):
                sp.wait_ge(unit_done, 2 * (B3 + 8))
                sp.wait_ge(act_lo, NK + 7 + s)
                load_y(X1, 8, 0, s)

            def pass1_turn(i, s):
                load_w(sp, B3 + 10 + s, 2, i)
                sp.wait_ge(pair3_free[s], i * 2 + 2)
                sp.wait_ge(a_stored[s], i * 16 + 16)
                sp.dma_start(row(a_d[ds(i * 2 + s, 1)]), acc_tile(i, s)).then_inc(a_stored[s], 16)

            with nc.sync.Fori(0, 3) as i:
                for s in range(2):
                    pass1_turn(i, s)
                    sp.wait_ge(act_lo, i * 2 + (NK + 9 + s))
                    load_y(X1, 8, i + 1, s)
            for s in range(2):
                pass1_turn(3, s)
            sp.wait_ge(sq_done, 16)
            for s in range(2):
                load_merge(0, s)

            def load_rows(i, s):
                sp.dma_start(acc_tile(i, s), a["x"][ds(i * (2 * P) + s * P, P), :]).then_inc(rows_in, 16)

            with nc.sync.Fori(0, 3) as i:
                for s in range(2):
                    load_w(sp, B3 + 18 + s, 2, i)
                    sp.wait_ge(m_lo, i * 4 + (2 * s + 2))
                    load_merge(i + 1, s)
                    load_rows(i, s)
            for s in range(2):
                load_w(sp, B3 + 24 + s, 0, 0)
            for s in range(2):
                sp.wait_ge(m_lo, 14 + 2 * s)
                load_rows(3, s)
            with nc.sync.Fori(0, 3) as i:
                for s in range(2):
                    load_w(sp, B3 + 26 + s, 2, i)
            for c in range(2):
                for t in range(NT):
                    sp.wait_ge(out_ready, 8 + NT * c + t + 1)
                    to = slice(c * HALF, (c + 1) * HALF)
                    sp.dma_start(out[t * P:(t + 1) * P, to], acc[:, t, to]).then_inc(out_stored, 16)
            sp.wait_ge(out_stored, 16 * 2 * NT)

        @block.gpsimd
        def _(pool):
            ch = Chain(pool, sq_done)
            pool.wait_ge(sdec_ready, 4 * NT)
            nc.gpsimd.memset(ms, 0.0).then_inc(y_sq, 1)

            def squares(X, k0, i, s):
                pool.wait_ge(gated, i * 2 + (k0 + s + 1))
                nc.gpsimd.tensor_tensor(part[:, s, :], tile(X, 1, i, s), tile(X, 1, i, s), ALU.mult).then_inc(y_sq, 1)
                pool.wait_ge(y_sq, i * 2 + (k0 + s + 2))
                ch.link(nc.gpsimd.tensor_tensor(ms, ms, part[:, s, :], ALU.add))

            for n0, X in ((0, X0), (8, X1)):
                for i in ch.loop(nc.gpsimd.Fori, 4, 2):
                    for s in range(2):
                        squares(X, n0, i, s)
                        low(pool, B3 + n0 + 2 + s, 2, i)
            pool.wait_ge(rms_ready, 1)
            with nc.gpsimd.Fori(0, 4) as i:
                for s in range(2):
                    pool.wait_ge(gateB_ready, i * 2 + (s + 1))
                    nc.gpsimd.tensor_tensor(gate[:, s, :], gate[:, s, :], ms, ALU.mult).then_inc(gr_ready, 1)
                    low(pool, B3 + 18 + s, 2, i)
            with nc.gpsimd.Fori(0, 3) as i:
                for s in range(2):
                    low(pool, B3 + 26 + s, 2, i)

        @block.scalar
        def _(act):
            def silu_and_high(X, q0, i, s):
                act.wait_ge(y_in[s], i * 32 + (16 * q0 + 32))
                nc.scalar.activation(tile(X, 0, i, s), tile(X, 0, i, s), ACT.Silu).then_inc(silu3, 1)
                act.wait_ge(gated, i * 2 + (q0 + s + 1))
                nc.scalar.activation(split_tile(X, 0, i, s), tile(X, 1, i, s), ACT.Identity,
                                     scale=C("ssd_gain", q0, q0 + 8)[:, ds(i * 2 + s, 1)]).then_inc(act_hi, 1)

            act.wait_ge(st_done, 4 * NT)
            for k in range(DVE_TILES, NK):
                act.wait_ge(o_in[k], 16)
                nc.scalar.activation(X1[:, 0, k, :], X1[:, 1, k, :].bitcast(f32), ACT.Copy).then_inc(act_hi, 1)
            with nc.scalar.Fori(0, 4) as i:
                for s in range(2):
                    act.wait_ge(gateA_in[s], i * 16 + 16)
                    nc.scalar.activation(acc_tile(i, s), acc_tile(i, s), ACT.Sigmoid,
                                         bias=C("b_gate", 0, 8)[:, ds(i * 2 + s, 1)]).then_inc(gateA_ready, 1)
                    silu_and_high(X0, 0, i, s)
                    high(act, B3 + 2 + s, 2, i)
            with nc.scalar.Fori(0, 4) as i:
                for s in range(2):
                    silu_and_high(X1, 8, i, s)
                    high(act, B3 + 10 + s, 2, i)
                    act.wait_ge(a_stored[s], i * 16 + 32)
                    nc.scalar.activation(acc_tile(i, s), pair3(s), ACT.Copy).then_inc(pair3_free[s], 2)
            act.wait_ge(ms_done, 1)
            nc.scalar.activation(ms, flat(M[:, 0:2, :]), ACT.Sqrt, bias=eps[:], scale=1.0 / (2 * DM)).then_inc(ms_rt, 1)

            def merged_high(i, s, h):
                act.wait_ge(acc_ready, i * 4 + (2 * s + h + 1))
                to = slice(h * HALF, (h + 1) * HALF)
                nc.scalar.activation(split_tile(X0, 0, i, s)[:, to], acc_tile(i, s)[:, to], ACT.Copy).then_inc(m_hi, 1)

            with nc.scalar.Fori(0, 4) as i:
                for s in range(2):
                    act.wait_ge(merge_in[s], i * 32 + 32)
                    nc.scalar.activation(gate[:, s, :], gate[:, s, :], ACT.Sigmoid,
                                         bias=C("b_gate", 8, 16)[:, ds(i * 2 + s, 1)]).then_inc(gateB_ready, 1)
                    merged_high(i, s, 0)
                    high(act, B3 + 18 + s, 2, i)
                    merged_high(i, s, 1)
            with nc.scalar.Fori(0, 3) as i:
                for s in range(2):
                    high(act, B3 + 26 + s, 2, i)

        @block.vector
        def _(dve):
            ch = Chain(dve, step3)

            def gate_and_low(X, q0, i, s):
                y, n = tile(X, 1, i, s), q0 + s + 1
                dve.wait_ge(silu3, i * 2 + n)
                nc.vector.tensor_tensor(y, y, tile(X, 0, i, s), ALU.mult).then_inc(gated, 1)
                dve.wait_ge(act_hi, i * 2 + (NK - DVE_TILES + n))
                dve.wait_ge(y_sq, i * 2 + (n + 1))
                nc.vector.scalar_tensor_tensor(split_tile(X, 1, i, s), y, C("ssd_gain", q0, q0 + 8)[:, ds(i * 2 + s, 1)],
                                               tile(X, 0, i, s), ALU.mult, ALU.subtract).then_inc(act_lo, 1)

            dve.wait_ge(st_done, 4 * NT)
            for k in range(NK):
                if k < DVE_TILES:
                    dve.wait_ge(o_in[k], 16)
                    ch.link(nc.vector.tensor_copy(X1[:, 0, k, :], X1[:, 1, k, :].bitcast(f32)))
                else:
                    dve.wait_ge(act_hi, k - DVE_TILES + 1)
                nc.vector.tensor_tensor(X1[:, 1, k, :], X1[:, 1, k, :].bitcast(f32), X1[:, 0, k, :].bitcast(f32),
                                        ALU.subtract).then_inc(act_lo, 1)
            with nc.vector.Fori(0, 4) as i:
                for s in range(2):
                    gate_and_low(X0, 0, i, s)
                    dve.wait_ge(gateA_ready, i * 2 + (s + 1))
                    dve.wait_ge(unit_done, i * 4 + 2 * (B3 + s + 1))
                    nc.vector.tensor_tensor(acc_tile(i, s), acc_tile(i, s), pair3(s), ALU.mult).then_inc(pair3_free[s], 2)
            with nc.vector.Fori(0, 4) as i:
                for s in range(2):
                    gate_and_low(X1, 8, i, s)
            dve.wait_ge(ms_rt, 1)
            nc.vector.reciprocal(ms, ms).then_inc(rms_ready, 1)
            for i in ch.loop(nc.vector.Fori, 4, 8):
                for s in range(2):
                    for h in range(2):
                        to = slice(h * HALF, (h + 1) * HALF)
                        sum_b = acc_tile(i, s)[:, to]
                        dve.wait_ge(unit_done, i * 4 + (2 * (B3 + 16 + s) + h + 1))
                        ch.link(nc.vector.tensor_tensor(sum_b, sum_b, F[:, 2 * s + h, :], ALU.add))
                        dve.sem_inc(pair3_free[s], 1)
                        dve.wait_ge(gr_ready, i * 2 + (s + 1))
                        ch.link(nc.vector.tensor_tensor(sum_b, sum_b, gate[:, s, to], ALU.mult))
                        dve.wait_ge(merge_in[s], i * 32 + 32)
                        nc.vector.tensor_tensor(sum_b, sum_b, part[:, s, to], ALU.add).then_inc(acc_ready, 1)
                        dve.wait_ge(m_hi, i * 4 + (2 * s + h + 1))
                        nc.vector.tensor_tensor(split_tile(X0, 1, i, s)[:, to], sum_b, tile(X0, 0, i, s)[:, to],
                                                ALU.subtract).then_inc(m_lo, 1)
            dve.wait_ge(rows_in, 16 * NT)
            for c in range(2):
                for t in range(NT):
                    if t < NT - 1:
                        dve.wait_ge(row_done, (NT - 1) * c + t + 1)
                    else:
                        dve.wait_ge(unit_done, 2 * (B3 + 28 + 4 * c))
                    to = acc[:, t, c * HALF:(c + 1) * HALF]
                    nc.vector.tensor_tensor(to, to, row_bank(t), ALU.add).then_inc(out_ready, 1)

        @block.tensor
        def _(pe):
            pe.sem_inc(out_ready, 8)

            def unit3(n, act, i, free=True, tiles=None):
                s = n % 2
                pe.wait_ge(w_hi, i * 2 + (B3 + n + 1))
                pe.wait_ge(w_lo, i * 2 + (B3 + n + 1))
                if free:
                    pe.wait_ge(pair3_free[s], i * 2 + 2 * (n // 2))
                for h in range(2):
                    if tiles is not None and h == 0:
                        for k in range(NK):
                            pe.wait_ge(act_lo, tiles + k + 1)
                            for wp, ap in ((0, 0), (0, 1), (1, 0)):
                                last = nc.tensor.matmul(F[:, 2 * s, :], whl[:, 1 - s, wp, k, :], act[:, ap, k, 0:HALF],
                                                        start=(k == 0 and wp == 0 and ap == 0), stop=(k == NK - 1 and wp == 1))
                        last.then_inc(unit_done, 1)
                    else:
                        matmuls(F[:, 2 * s + h, :], 1 - s, act, h).then_inc(unit_done, 1)

            unit3(0, X1, 0, free=False, tiles=0)
            pe.wait_ge(half_taken, 8 * NT + 2)
            unit3(1, X1, 0, free=False)
            with nc.tensor.Fori(0, 3) as i:
                for s in range(2):
                    unit3(2 + s, X1, i)
            unit3(8, X0, 0, tiles=8)
            unit3(9, X0, 0)
            with nc.tensor.Fori(0, 3) as i:
                for s in range(2):
                    unit3(10 + s, X0, i)
            pe.wait_ge(act_lo, 24)
            pe.wait_ge(sq_done, 16)
            for h in range(2):
                last = nc.tensor.matmul(M[:, h, :], C("ones"), ms[:, h * HALF:(h + 1) * HALF], start=True, stop=True)
            last.then_inc(ms_done, 1)
            for n in (16, 17):
                unit3(n, X1, 0)
            with nc.tensor.Fori(0, 3) as i:
                for s in range(2):
                    unit3(18 + s, X1, i)
            with nc.tensor.Fori(0, 2) as c:
                for kp in range(4):
                    n = 24 + kp
                    slot = (n + 1) % 2
                    pe.wait_ge(w_hi, c * 4 + (B3 + n + 1))
                    pe.wait_ge(w_lo, c * 4 + (B3 + n + 1))
                    w_half = whl[:, slot].rearrange("p w k c -> p w (k c)")
                    for t0, k in ((0, 2 * kp), (0, 2 * kp + 1), (4, 2 * kp), (4, 2 * kp + 1)):
                        pe.wait_ge(m_lo, 2 * k + 2)
                        if k == 0 and t0 == 4:
                            for p in range(2):
                                pe.wait_ge(pair3_free[p], 24)
                        for t in range(t0, t0 + 4):
                            if k == 0:
                                pe.wait_ge(out_ready, c * 8 + (t + 1))
                            for wp, ap in ((0, 0), (1, 0), (0, 1)):
                                last = nc.tensor.matmul(row_bank(t), X0[:, ap, k, t * P:(t + 1) * P],
                                                        w_half[:, wp, (k % 2) * HALF:(k % 2 + 1) * HALF],
                                                        start=(k == 0 and wp == 0 and ap == 0), stop=(k == NK - 1 and ap == 1))
                            if k == NK - 1 and t < NT - 1:
                                last.then_inc(row_done, 1)
                    last.then_inc(unit_done, 2)


def kernel(**inputs):
    import numpy as np
    import concourse.bacc as bacc
    from concourse.bass_utils import run_bass_kernel_spmd

    def cols(v):
        return np.ascontiguousarray(v.reshape(-1, P).T)

    def rows(v):
        return np.broadcast_to(v, (P, v.size))

    w = {n: np.ascontiguousarray(v[0], dtype=np.float32) for n, v in inputs.items()}
    s = np.arange(P)
    parts = {
        "conv_w": w["conv_w"].reshape(4, NX, P).transpose(2, 1, 0).reshape(P, NX * 4),
        "conv_b": cols(w["conv_b"]), "b_gate": cols(w["b_gate"]), "ssd_gain": cols(w["ssd_norm_gain"]),
        "d_skip": cols(np.repeat(w["d_skip"], HD)),
        "q_gain": cols(np.tile(w["q_norm_gain"], 2)), "k_gain": cols(np.tile(w["k_norm_gain"], 2)),
        "dt_bias": rows(w["dt_bias"]), "a_log": rows(w["a_log"]),
        "sinks": rows(w["attn_sinks"]),
        "pad_mask": np.where(np.arange(NT)[None, :] == 0, NEG, 0.0) * (s[:, None] < CH),
        "ident": np.eye(P), "tri": s[:, None] <= s[None, :],
        "ones": np.ones((P, P)), "head_ones": s[:, None] // HD == s[None, :] // HD, "head_sel": s[:, None] // HD == np.arange(2)[None, :],
    }
    consts = np.concatenate([np.asarray(parts[n], np.float32) for n, _ in CONST_COLS], axis=1)
    half = HD // 2
    inv = np.float32(10000.0) ** (-np.arange(half, dtype=np.float32) / half)
    ang = np.arange(T, dtype=np.float32)[None, :] * inv[:, None]
    cos = np.tile(np.cos(ang), (4, 1)).astype(np.float32)
    sin = np.tile(np.concatenate([np.sin(ang), -np.sin(ang)]), (2, 1)).astype(np.float32)

    def units(m):
        return m.reshape(NK, P, -1, P).transpose(2, 1, 0, 3).reshape(-1, P, NK * P)

    def row_units(m):
        return m.reshape(NK // 2, 2, P, 2, HALF).transpose(3, 0, 2, 1, 4).reshape(-1, P, NK * P)

    q, k, v, z_a, z_s, xbc, dt, g = np.split(w["w_in"], np.cumsum([1024, 256, 256, 1024, 2048, NX * P, NHS]), axis=1)
    q = q.reshape(DM, 2, 2, 4, HD).transpose(0, 1, 3, 2, 4).reshape(DM, DM)
    dt = np.concatenate([dt, np.zeros((DM, P - NHS), np.float32)], axis=1)
    per_tile = np.concatenate([units(z_s).reshape(NT, 2, P, -1), units(g).reshape(NT, 2, P, -1)], axis=1)
    w_units = np.concatenate([units(dt), units(v), units(k), units(q), units(xbc), units(z_a), per_tile.reshape(4 * NT, P, -1),
                              units(w["w_attn_proj"]), units(w["w_ssd_proj"][:DM]), units(w["w_ssd_proj"][DM:]), row_units(w["w_out"])])
    assert len(w_units) == UNITS
    arrays = {"x": w["x"], "w_units": w_units, "consts": consts, "gain": np.ascontiguousarray(rows(w["norm_gain"])),
              "cos": cos, "sin": sin}
    nc = bacc.Bacc("TRN2", target_bir_lowering=False, num_devices=1)
    aps = {n: nc.dram_tensor(n, v.shape, mybir.dt.float32, kind="ExternalInput").ap() for n, v in arrays.items()}
    out = nc.dram_tensor("out", (T, DM), mybir.dt.float32, kind="ExternalOutput").ap()
    build(nc, aps, out)
    r = run_bass_kernel_spmd(nc, [arrays], core_ids=[0])
    return r.results[0]["out"].reshape(1, T, DM)
```
